# Optimizing a Trainium2 kernel written in Bass

```python
import jax, jax.numpy as jnp
from jax import lax
import numpy as np

D_MODEL = 1024
BATCH = 1
SEQ = 2048
DEPTH = 1

D_CONV = D_MODEL
CONV_WIDTH = 3
HEAD_DIM = 64
N_HEADS = D_MODEL // HEAD_DIM
N_KV_HEADS = 2
GROUP = N_HEADS // N_KV_HEADS
D_ATTN = N_HEADS * HEAD_DIM
D_KV = N_KV_HEADS * HEAD_DIM
WINDOW = 128
BLOCK = WINDOW
ROPE_THETA = 10000.0
RMS_EPS = 1e-6
SPLITS = (D_CONV, D_CONV, D_CONV, D_CONV, D_ATTN, D_KV, D_KV, D_ATTN, D_MODEL, D_MODEL)
D_IN = int(sum(SPLITS))
SPLIT_IDX = [int(s) for s in np.cumsum(SPLITS)[:-1]]

kernel_name = "hybrid_shortconv_swa_sink_gated_merge"

def rmsnorm(x, g):
    xf = x.astype(jnp.float32)
    y = xf * lax.rsqrt(jnp.mean(xf * xf, axis=-1, keepdims=True) + RMS_EPS)
    return (y * g.astype(jnp.float32)).astype(x.dtype)

def short_gated_conv(xc, bg, cg, w_conv):
    u = cg * xc
    t = u.shape[1]
    u_pad = jnp.pad(u, ((0, 0), (CONV_WIDTH - 1, 0), (0, 0)))
    y = w_conv[0] * u_pad[:, 0:t]
    for tap in range(1, CONV_WIDTH):
        y = y + w_conv[tap] * u_pad[:, tap:tap + t]
    return bg * y

def rope(z, positions):
    inv_freq = ROPE_THETA ** (-jnp.arange(0, HEAD_DIM, 2, dtype=jnp.float32) / HEAD_DIM)
    ang = positions.astype(jnp.float32)[:, None] * inv_freq[None, :]
    cos = jnp.cos(ang)[:, None, :]
    sin = jnp.sin(ang)[:, None, :]
    zf = z.astype(jnp.float32)
    z1, z2 = zf[..., :HEAD_DIM // 2], zf[..., HEAD_DIM // 2:]
    out = jnp.concatenate([z1 * cos - z2 * sin, z2 * cos + z1 * sin], axis=-1)
    return out.astype(z.dtype)

def sliding_window_attention(q, k, v, sinks):
    b, t = q.shape[0], q.shape[1]
    nblk = t // BLOCK
    qb = q.reshape(b, nblk, BLOCK, N_KV_HEADS, GROUP, HEAD_DIM).transpose(1, 0, 2, 3, 4, 5)

    def band(z):
        zb = z.reshape(b, nblk, BLOCK, N_KV_HEADS, HEAD_DIM)
        prev = jnp.concatenate([jnp.zeros_like(zb[:, :1]), zb[:, :-1]], axis=1)
        return jnp.concatenate([prev, zb], axis=2).transpose(1, 0, 2, 3, 4)

    kb, vb = band(k), band(v)
    qi = jnp.arange(BLOCK)[:, None]
    kj = jnp.arange(2 * BLOCK)[None, :]
    in_band = (kj > qi) & (kj <= qi + BLOCK)
    sink = sinks.astype(jnp.float32).reshape(N_KV_HEADS, GROUP, 1, 1)
    scale = HEAD_DIM ** -0.5

    def one_block(args):
        blk, qblk, kblk, vblk = args
        logits = jnp.einsum('bqkgd,bskd->bkgqs', qblk, kblk).astype(jnp.float32) * scale
        valid = in_band & (kj >= BLOCK - blk * BLOCK)
        logits = jnp.where(valid, logits, -jnp.inf)
        m = jnp.maximum(jnp.max(logits, axis=-1, keepdims=True), sink)
        p = jnp.exp(logits - m)
        denom = jnp.sum(p, axis=-1, keepdims=True) + jnp.exp(sink - m)
        probs = (p / denom).astype(vblk.dtype)
        return jnp.einsum('bkgqs,bskd->bqkgd', probs, vblk)

    out = lax.map(one_block, (jnp.arange(nblk), qb, kb, vb))
    return out.transpose(1, 0, 2, 3, 4, 5).reshape(b, t, D_ATTN)

def hybrid_layer(x, g_pre, g_post, w_in, w_conv, sinks, w_proj_conv, w_proj_attn, w_out):
    b, t, _ = x.shape
    h = rmsnorm(x, g_pre)
    proj = jnp.einsum('btd,de->bte', h, w_in)
    xc, bg, cg, zc, q, k, v, za, ga, gb = jnp.split(proj, SPLIT_IDX, axis=-1)

    ua = jax.nn.silu(zc) * short_gated_conv(xc, bg, cg, w_conv)
    ya = jnp.einsum('btc,cd->btd', ua, w_proj_conv)

    positions = jnp.arange(t)
    q = rope(q.reshape(b, t, N_HEADS, HEAD_DIM), positions)
    k = rope(k.reshape(b, t, N_KV_HEADS, HEAD_DIM), positions)
    v = v.reshape(b, t, N_KV_HEADS, HEAD_DIM)
    ub = jax.nn.silu(za) * sliding_window_attention(q, k, v, sinks)
    yb = jnp.einsum('bta,ad->btd', ub, w_proj_attn)

    merged = jax.nn.sigmoid(ga) * ya + jax.nn.sigmoid(gb) * yb
    y = jnp.einsum('btd,de->bte', merged, w_out)
    return x + rmsnorm(y, g_post)

def setup_inputs(seed: int = 0) -> dict:
    key = jax.random.key(seed)
    ks = jax.random.split(key, 10)
    f32 = jnp.float32
    x = jax.random.normal(ks[0], (BATCH, SEQ, D_MODEL), f32)
    g_pre = 1.0 + 0.05 * jax.random.normal(ks[1], (DEPTH, D_MODEL), f32)
    g_post = 1.0 + 0.05 * jax.random.normal(ks[2], (DEPTH, D_MODEL), f32)
    w_in = jax.random.normal(ks[3], (DEPTH, D_MODEL, D_IN), f32) * D_MODEL ** -0.5
    w_conv = jax.random.normal(ks[4], (DEPTH, CONV_WIDTH, D_CONV), f32) * CONV_WIDTH ** -0.5
    sinks = 0.5 * jax.random.normal(ks[5], (DEPTH, N_HEADS), f32)
    w_proj_conv = jax.random.normal(ks[6], (DEPTH, D_CONV, D_MODEL), f32) * D_CONV ** -0.5
    w_proj_attn = jax.random.normal(ks[7], (DEPTH, D_ATTN, D_MODEL), f32) * D_ATTN ** -0.5
    w_out = jax.random.normal(ks[8], (DEPTH, D_MODEL, D_MODEL), f32) * D_MODEL ** -0.5
    return {"x": x, "g_pre": g_pre, "g_post": g_post, "w_in": w_in, "w_conv": w_conv,
            "sinks": sinks, "w_proj_conv": w_proj_conv, "w_proj_attn": w_proj_attn, "w_out": w_out}

def reference(x, g_pre, g_post, w_in, w_conv, sinks, w_proj_conv, w_proj_attn, w_out):
    for layer in range(DEPTH):
        x = hybrid_layer(x, g_pre[layer], g_post[layer], w_in[layer], w_conv[layer], sinks[layer],
                         w_proj_conv[layer], w_proj_attn[layer], w_out[layer])
    return x


_drawn_inputs = setup_inputs


def setup_inputs(seed=0):
    import zlib

    import numpy as np

    out = dict(_drawn_inputs(seed))
    spreads = {}
    factors = {'sinks': 8.0}
    for name, (base, spread) in spreads.items():
        noise = np.random.default_rng([zlib.crc32(name.encode()), seed]).standard_normal(out[name].shape)
        drawn = base * np.exp(spread * noise) if base else spread * noise
        out[name] = __import__('jax').numpy.asarray(drawn.astype(out[name].dtype))
    for name, factor in factors.items():
        out[name] = (out[name] * factor).astype(out[name].dtype)
    return out
```

```python
from contextlib import ExitStack

import numpy as np

import concourse.bass as bass
from concourse import mybir

F32 = mybir.dt.float32
F32R = mybir.dt.float32r
ACT = mybir.ActivationFunctionType
ALU = mybir.AluOpType

P = 128
SEQ, D = 2048, 1024
KT = D // P
T = 512
NQ = SEQ // T
TT = T // P
HEADS, HD, KVH = 16, 64, 2
UNIT_HEADS = 4
GROUPS = HEADS // UNIT_HEADS
UNITS = TT * GROUPS
EPS = 1e-6
MASKED = -1e30

KV, Q, ZA, GATES, CONV, YA, YB, Y, PAIRS = 0, 1, 5, 9, 17, 33, 37, 41, 45
JOBS = 2 * PAIRS
LEAD = 2
ROPED = 1 + HEADS // 2


def build(nc, x, wjobs, g_pre, g_post, w_conv, sinks, tables, masks, out):
    ctx = ExitStack()
    with ctx:
        def sbuf(name, shape, dtype=F32):
            return ctx.enter_context(nc.sbuf_tensor(name, shape, dtype))

        def psum(name, shape):
            return ctx.enter_context(nc.psum_tensor(name, shape, F32))

        def sem(name):
            return ctx.enter_context(nc.semaphore(name))

        h_hi = sbuf("h_hi", [P, KT, T], F32R)
        h_lo = sbuf("h_lo", [P, KT, T], F32R)
        qu = sbuf("qu", [P, HEADS, T], F32R)
        m_hi = sbuf("m_hi", [P, KT, T], F32R)
        m_lo = sbuf("m_lo", [P, KT, T], F32R)
        za = sbuf("za", [P, KT, T])
        gates = sbuf("gates", [P, 2 * KT, T])
        ga, gb = gates[:, 0:KT, :], gates[:, KT:2 * KT, :]
        w_raw = sbuf("w_raw", [P, 2, D])
        w_hi = [sbuf(f"w_hi{i}", [P, KT, P], F32R) for i in range(2)]
        w_lo = [sbuf(f"w_lo{i}", [P, KT, P], F32R) for i in range(2)]
        kk = sbuf("kk", [P, KVH, 2, P + T], F32R)
        vv = sbuf("vv", [P, 1 + TT, KVH, 2 * HD], F32R)
        rope = sbuf("rope", [P, 2, T])
        band = sbuf("band", [P, 2, P])
        mask = sbuf("mask", [P, 2, P])
        ident = sbuf("ident", [P, P])
        gpre = sbuf("gpre", [P, D])
        taps = sbuf("taps", [P, KT, 3])
        sink = sbuf("sink", [P, HEADS])
        halo = sbuf("halo", [P, KT, 2])
        otmp = sbuf("otmp", [P, 2, P])
        att = sbuf("att", [P, 2, P])
        rowmax = sbuf("rowmax", [P, 2, UNIT_HEADS])
        negmax = sbuf("negmax", [P, 2, UNIT_HEADS])
        sinkd = sbuf("sinkd", [P, 2, UNIT_HEADS])
        rowsum = sbuf("rowsum", [P, 2, UNIT_HEADS])
        denom = sbuf("denom", [P, 2, UNIT_HEADS])
        rden = sbuf("rden", [P, 2, UNIT_HEADS])
        mean = sbuf("mean", [P, 2 * TT])
        msq = sbuf("msq", [P, 2 * TT])
        rstd = sbuf("rstd", [P, 2 * TT])
        root_consts = sbuf("root_consts", [P, 2])
        carrier = sbuf("carrier", [P, 1])
        work = sbuf("work", [P, 4 * T + 2])

        def f32(ap):
            return ap.bitcast(F32)

        prob = [work[:, i * 2 * T:(i + 1) * 2 * T].rearrange("p (h k) -> p h k", h=UNIT_HEADS)
                for i in range(2)]
        c_in, c_y, c_gate = (work[:, i * T:(i + 1) * T] for i in range(3))
        c_u = work[:, 3 * T:4 * T + 2]
        xs = gpost = work[:, 0:D]
        v_raw = gb[:, 0, :]
        rot = [gb[:, 1 + i, :] for i in range(2)]
        qr = [gb[:, (3, 6)[i], :] for i in range(2)]
        silu_tmp = [gb[:, 4 + i, :] for i in range(2)]

        def token_rows(tensor):
            return tensor.rearrange("p (t a) n -> p t (a n)", t=TT)

        x_first, x_last, y_out = token_rows(za[:, :, :]), token_rows(ga), token_rows(gb)
        y_squares = m_lo[:, 0:2, :].rearrange("p a n -> p (a n)")
        y_scaled_row = work[:, D:2 * D]
        pt_hi = [m_hi[:, 2 * i:2 * i + 2, :] for i in range(2)]
        pt_lo = [m_lo[:, 2 * i:2 * i + 2, :] for i in range(2)]

        gemm = [psum(f"gemm{i}", [P, T]) for i in range(2)]
        s_ps = psum("s_ps", [P, UNIT_HEADS, 2 * P])
        t_ps = psum("t_ps", [P, KT, P])
        o_ps = psum("o_ps", [P, UNIT_HEADS, P])
        v_ps = psum("v_ps", [P, TT, KVH, HD])
        s_flat = s_ps[:, :, :].rearrange("p h k -> p (h k)")
        t_flat = t_ps[:, :, :].rearrange("p h k -> p (h k)")
        s_tiles = s_flat.rearrange("p (t k) -> p t k", k=P)

        gain_loaded = sem("gain_loaded")
        consts_loaded = sem("consts_loaded")
        kv_zeroed = sem("kv_zeroed")
        root_consts_set = sem("root_consts_set")
        w_loaded = [sem(f"w_loaded{i}") for i in range(2)]
        w_hi_ready = sem("w_hi_ready")
        w_lo_ready = sem("w_lo_ready")
        half_job = sem("half_job")
        bank_free = [sem(f"bank_free{i}") for i in range(2)]
        x_first_loaded = [sem(f"x_first_loaded{t}") for t in range(TT)]
        xs_loaded = sem("xs_loaded")
        x_mean = sem("x_mean")
        x_msq = sem("x_msq")
        x_rstd = sem("x_rstd")
        x_normed = sem("x_normed")
        h_transposed = sem("h_transposed")
        h_hi_ready = sem("h_hi_ready")
        h_ready = sem("h_ready")
        rope_loaded = sem("rope_loaded")
        kv_carried = sem("kv_carried")
        rot_ready = sem("rot_ready")
        rot_scaled = sem("rot_scaled")
        roped = sem("roped")
        rope_hi = sem("rope_hi")
        rope_lo = sem("rope_lo")
        v_transposed = sem("v_transposed")
        v_hi_ready = sem("v_hi_ready")
        v_ready = sem("v_ready")
        gate_sig = sem("gate_sig")
        scores_ready = sem("scores_ready")
        scores_used = sem("scores_used")
        mask_full = sem("mask_full")
        negmax_ready = sem("negmax_ready")
        exp_done = sem("exp_done")
        denom_ready = sem("denom_ready")
        rden_ready = sem("rden_ready")
        probs_ready = sem("probs_ready")
        pt_ready = sem("pt_ready")
        pt_hi_ready = sem("pt_hi_ready")
        pt_lo_ready = sem("pt_lo_ready")
        o_ready = sem("o_ready")
        o_moved = sem("o_moved")
        o_added = sem("o_added")
        ub_gated = sem("ub_gated")
        ub_hi_ready = sem("ub_hi_ready")
        ub_ready = sem("ub_ready")
        halo_in = sem("halo_in")
        tap_done = sem("tap_done")
        z_sig = sem("z_sig")
        ua_mixed = sem("ua_mixed")
        ua_hi_ready = sem("ua_hi_ready")
        ua_ready = sem("ua_ready")
        merge_sig = sem("merge_sig")
        merged = sem("merged")
        m_hi_ready = sem("m_hi_ready")
        m_ready = sem("m_ready")
        tail_loaded = sem("tail_loaded")
        y_transposed = sem("y_transposed")
        y_mean = sem("y_mean")
        y_msq = sem("y_msq")
        y_rstd = sem("y_rstd")
        y_scaled = sem("y_scaled")
        y_summed = sem("y_summed")
        out_stored = sem("out_stored")
        N_CONSTS = 4 * 16

        def done(q, pair, k):
            return q * 2 * JOBS + pair * 4 + 2 * k + 2

        def freed(q, pair):
            return q * PAIRS + pair + 1

        def unit(q, u):
            return q * UNITS + u + 1

        def slots():
            return ((s, s % 2) for s in range(-LEAD, 0))

        def steps(i):
            last = isinstance(i, int)
            for g in range(GROUPS):
                yield (g, GATES + 2 * i + (g + LEAD) // 2, not (last and g + LEAD >= GROUPS),
                       not (last and g + 1 >= GROUPS))

        block = ctx.enter_context(nc.Block())

        @block.sync
        def _(sp):
            for t in range(TT):
                sp.dma_start(x_first[:, t, :], x[t * P:(t + 1) * P, :]).then_inc(x_first_loaded[t], 16)
                if t == 0:
                    sp.dma_start(gpre[:, :], g_pre.broadcast_to([P, D])).then_inc(gain_loaded, 16)
                    sp.dma_start(ident[:, :], masks[:, 0:P]).then_inc(gain_loaded, 16)
            for k in range(2):
                sp.dma_start(w_raw[:, k, :], wjobs[k]).then_inc(w_loaded[k], 16)
            sp.dma_start(band[:, :, :], masks[:, P:3 * P].rearrange("p (a k) -> p a k", a=2)).then_inc(consts_loaded, 16)
            sp.dma_start(mask[:, :, :], masks[:, 3 * P:5 * P].rearrange("p (a k) -> p a k", a=2)).then_inc(consts_loaded, 16)
            sp.dma_start(taps[:, :, :], w_conv).then_inc(consts_loaded, 16)
            sp.dma_start(sink[:, :], sinks.broadcast_to([P, HEADS])).then_inc(consts_loaded, 16)

            def load_pair(q, pair, nxt):
                for k in range(2):
                    sp.wait_ge(w_lo_ready, done(q, pair, k))
                    sp.dma_start(w_raw[:, k, :], wjobs[2 * nxt + k]).then_inc(w_loaded[k], 16)

            def loads(q, first, end):
                with sp.Fori(first, end) as pair:
                    load_pair(q, pair, pair + 1)

            def load_rope(q):
                sp.dma_start(rope[:, :, :], tables[q].rearrange("p (a t) -> p a t", a=2)).then_inc(rope_loaded, 16)

            def quarter(q, last):
                loads(q, 0, YA)
                if not last:
                    sp.wait_ge(roped, (q + 1) * ROPED)
                    load_rope(q + 1)
                if last:
                    loads(q, YA, Y + 1)
                else:
                    with sp.Fori(0, TT) as t:
                        load_pair(q, YA + 2 * t, YA + 2 * t + 1)
                        sp.wait_ge(ua_ready, KT * (q + 1))
                        sp.wait_ge(h_transposed, TT * (q + 1) + t)
                        sp.dma_start(xs, x[bass.ds((q + 1) * T + t * P, P), :]).then_inc(xs_loaded, 16)
                        load_pair(q, YA + 2 * t + 1, YA + 2 * t + 2)
                    load_pair(q, Y, Y + 1)
                sp.wait_ge(m_ready, KT * (q + 1))
                if not last:
                    sp.wait_ge(h_transposed, TT * (q + 2))
                sp.dma_start(x_last, x[bass.ds(q * T, T), :].rearrange("(t p) d -> p t d", p=P)).then_inc(tail_loaded, 16)
                sp.dma_start(gpost, g_post.broadcast_to([P, D])).then_inc(tail_loaded, 16)
                loads(q, Y + 1, PAIRS - 1)
                if not last:
                    load_pair(q, PAIRS - 1, 0)

            load_rope(0)
            with sp.Fori(0, NQ - 1) as q:
                quarter(q, False)
            quarter(NQ - 1, True)

        @block.tensor
        def _(pe):
            def job(q, pair, k, hi, lo, tiles=None, per_quarter=KT, first=False):
                if tiles is not None:
                    pe.wait_ge(tiles, per_quarter * (q + 1) - 1)
                if not first:
                    pe.wait_ge(bank_free[k], freed(q, pair) - 1)
                for kt in range(KT):
                    if kt % (KT // 2) == 0:
                        pe.wait_ge(w_lo_ready, done(q, pair, k) - 1 + kt // (KT // 2))
                    if kt == KT - 1 and tiles is not None:
                        pe.wait_ge(tiles, per_quarter * (q + 1))
                    for n, (w, moving) in enumerate(((w_lo[k], hi), (w_hi[k], lo), (w_hi[k], hi))):
                        ins = nc.tensor.matmul(gemm[k][:, :], w[:, kt, :], moving[:, kt, :],
                                               start=kt == 0 and n == 0, stop=kt == KT - 1 and n == 2)
                    if kt % (KT // 2) == KT // 2 - 1:
                        ins.then_inc(half_job, 1)

            def jobs(q, first, end, *operand):
                with pe.Fori(first, end) as pair:
                    for k in range(2):
                        job(q, pair, k, *operand)

            h, m = (h_hi, h_lo), (m_hi, m_lo)
            ub = (qu[:, 0:HEADS:2, :], qu[:, 1:HEADS:2, :])

            def transpose_h(ready, src, dst, read=0):
                pe.wait_ge(x_normed, ready)
                if read:
                    pe.wait_ge(h_ready, read)
                for c in range(KT):
                    ins = nc.tensor.transpose(dst[:, c, :], src[:, c * P:(c + 1) * P], ident[:, :])
                ins.then_inc(h_transposed, 1)

            def scores(q, u):
                b, g = divmod(u, GROUPS)
                if u == 0:
                    pe.wait_ge(rope_lo, (q + 1) * ROPED)
                if u > 0:
                    pe.wait_ge(scores_used, unit(q, u) - 1)
                for head in range(UNIT_HEADS):
                    for part in (1, 0):
                        ins = nc.tensor.matmul(s_ps[:, head, :], qu[:, UNIT_HEADS * g + head, b * P:(b + 1) * P],
                                               kk[:, g // 2, part, b * P:(b + 2) * P], start=part == 1, stop=part == 0)
                ins.then_inc(scores_ready, 1)

            def transpose_p(q, u):
                pe.wait_ge(probs_ready, unit(q, u))
                for part in range(2):
                    for head in range(UNIT_HEADS):
                        ins = nc.tensor.transpose(t_ps[:, UNIT_HEADS * part + head, :],
                                                  prob[u % 2][:, head, part * P:(part + 1) * P], ident[:, :])
                ins.then_inc(pt_ready, 1)

            def values(q, u):
                b, g = divmod(u, GROUPS)
                pe.wait_ge(pt_lo_ready, unit(q, u))
                if u > 0:
                    pe.wait_ge(o_added, unit(q, u) - 1)
                if u == 0:
                    pe.wait_ge(v_ready, q + 1)
                for n in range(4):
                    part, pt = n // 2, (pt_lo, pt_hi)[n % 2][u % 2]
                    ins = nc.tensor.matmul(o_ps[:, :, :].rearrange("p h t -> p (h t)"), vv[:, b + part, g // 2, :],
                                           pt[:, part, :], start=n == 0, stop=n == 3)
                ins.then_inc(o_ready, 1)

            def transpose_y(n, t, dst):
                for c in range(KT):
                    ins = nc.tensor.transpose(dst[:, c, :], za[:, c, t * P:(t + 1) * P], ident[:, :])
                ins.then_inc(y_transposed, 1)

            def head(q, before):
                pe.wait_ge(h_ready, TT * (q + 1))
                for k in range(2):
                    job(q, KV, k, *h, first=before is None)
                if before is None:
                    jobs(q, Q, ZA, *h)
                else:
                    for t in range(TT):
                        job(q, Q + t, 0, *h)
                        if t > 0:
                            pe.wait_ge(y_scaled, before * TT + t)
                        transpose_y(before * TT + t, t, t_ps)
                        job(q, Q + t, 1, *h)
                pe.wait_ge(bank_free[1], freed(q, KV))
                for b in range(TT):
                    ins = nc.tensor.transpose(v_ps[:, b, :, :].rearrange("p g d -> p (g d)"),
                                              v_raw[:, b * P:(b + 1) * P], ident[:, :])
                ins.then_inc(v_transposed, 1)

            def quarter(q, last):
                jobs(q, ZA, GATES, *h)
                for s in range(-LEAD, UNITS):
                    if s + LEAD < UNITS:
                        scores(q, s + LEAD)
                    if s >= 0:
                        values(q, s)
                    if 0 <= s + 1 < UNITS:
                        transpose_p(q, s + 1)
                    job(q, GATES + (s + LEAD) // 2, s % 2, *h)
                jobs(q, CONV + 1, YA, *h)
                for first, operand in ((YA, (*m, ua_ready)), (YB, (*ub, ub_ready, UNITS))):
                    if last:
                        jobs(q, first, first + KT // 2, *operand)
                    else:
                        with pe.Fori(0, TT // 2) as i:
                            job(q, first + 2 * i, 0, *operand)
                            job(q, first + 2 * i, 1, *operand)
                            job(q, first + 2 * i + 1, 0, *operand)
                            transpose_h(TT * (q + 1) + (first - YA) // 2 + i + 1, xs, t_ps)
                            job(q, first + 2 * i + 1, 1, *operand)
                jobs(q, Y, PAIRS, *m, m_ready)
                if not last:
                    head(q + 1, q)
                    return
                for k in range(2):
                    pe.wait_ge(bank_free[k], freed(q, PAIRS - 1))
                for t in range(TT):
                    if t >= 2:
                        pe.wait_ge(y_scaled, q * TT + t - 1)
                    transpose_y(q * TT + t, t, (s_tiles, t_ps)[t % 2])

            pe.wait_ge(gain_loaded, 2 * 16)
            for t in range(TT):
                transpose_h(t + 1, x_first[:, t, :], (t_ps, s_tiles)[t % 2], max(t - 1, 0))
            head(0, None)
            with pe.Fori(0, NQ - 1) as q:
                quarter(q, False)
            quarter(NQ - 1, True)

        @block.scalar
        def _(act):
            def copy(dst, src):
                return nc.scalar.activation(dst, src, ACT.Copy)

            def rotate(q, pair, k):
                act.wait_ge(half_job, done(q, pair, k))
                for a in range(4):
                    b = a ^ 1
                    ins = copy(rot[k][32 * b:32 * b + 32, :], gemm[k][32 * a:32 * a + 32, :])
                ins.then_inc(rot_ready, 1)

            def q_hi(q, n, k, head):
                act.wait_ge(roped, q * ROPED + n + 1)
                copy(qu[0:HD, head, :], qr[k][0:HD, :])
                copy(qu[HD:P, head + 1, :], qr[k][HD:P, :]).then_inc(rope_hi, 1)

            def exps(q, u, k):
                act.wait_ge(negmax_ready, unit(q, u))
                for head in range(UNIT_HEADS):
                    nc.scalar.activation(prob[k][:, head, :], prob[k][:, head, :], ACT.Exp,
                                         bias=negmax[:, k, head:head + 1], accum_out=rowsum[:, k, head:head + 1])
                nc.scalar.activation(sinkd[:, k, :], sinkd[:, k, :], ACT.Exp).then_inc(exp_done, 1)

            def split_p(q, u, k):
                act.wait_ge(pt_ready, unit(q, u))
                copy(pt_hi[k], t_flat.rearrange("p (a n) -> p a n", a=2)).then_inc(pt_hi_ready, 1)

            def move_o(q, u):
                act.wait_ge(o_ready, unit(q, u))
                copy(otmp[0:HD, :, :], o_ps[HD:P, 0:UNIT_HEADS:2, :])
                copy(otmp[HD:P, :, :], o_ps[0:HD, 1:UNIT_HEADS:2, :]).then_inc(o_moved, 1)

            def ub_hi(q, u, b, g):
                act.wait_ge(ub_gated, unit(q, u))
                copy(qu[:, UNIT_HEADS * g:UNIT_HEADS * (g + 1):2, bass.ds(b * P, P)], att[:, :, :])\
                    .then_inc(ub_hi_ready, 1)

            def merge_sigmoid(row):
                nc.scalar.activation(gates[:, row, :], gates[:, row, :], ACT.Sigmoid).then_inc(merge_sig, 1)

            def yb_hi(q, tile):
                act.wait_ge(merged, q * KT + tile + 1)
                act.wait_ge(half_job, done(q, YB, 0))
                copy(m_hi[:, tile, :], gb[:, tile, :]).then_inc(m_hi_ready, 1)

            def input_squares(n):
                act.wait_ge(xs_loaded, 16 * (n - TT + 1))
                act.wait_ge(h_ready, n)
                nc.scalar.activation(t_flat, xs, ACT.Square, scale=D ** -0.5, accum_out=mean[:, 0:1]).then_inc(x_mean, 1)

            def input_hi(n, t, src):
                act.wait_ge(h_transposed, n + 1)
                copy(h_hi[:, :, bass.ds(t * P, P)], src).then_inc(h_hi_ready, 1)

            def squares_y(n, src, dst, column):
                act.wait_ge(y_transposed, n + 1)
                nc.scalar.activation(dst, src, ACT.Square, scale=D ** -0.5,
                                     accum_out=mean[:, column:column + 1]).then_inc(y_mean, 1)

            def store_y(n, row):
                act.wait_ge(y_summed, n + 1)
                act.dma_start(out[bass.ds(n * P, P), :], row).then_inc(out_stored, 16)

            def head(q, before):
                rotate(q, KV, 0)
                act.wait_ge(roped, q * ROPED + 1)
                act.wait_ge(kv_carried, q + 1)
                for g in range(KVH):
                    for half in range(2):
                        ins = copy(kk[HD * half:HD * (half + 1), g, 0, P:P + T], qr[0][HD * g:HD * (g + 1), :])
                ins.then_inc(rope_hi, 1)
                act.wait_ge(half_job, done(q, KV, 1))
                copy(v_raw, gemm[1][:, :]).then_inc(bank_free[1], 1)
                with act.Fori(0, TT) as i:
                    rotate(q, Q + i, 0)
                    if before is not None:
                        squares_y(before * TT + i, t_flat, y_squares, TT)
                    q_hi(q, 1 + 2 * i, 0, 4 * i)
                    rotate(q, Q + i, 1)
                    q_hi(q, 2 + 2 * i, 1, 4 * i + 2)
                    if before is not None:
                        store_y(before * TT + i, x_last[:, i, :])
                act.wait_ge(v_transposed, q + 1)
                copy(vv[:, 1:1 + TT, :, 0:HD], v_ps[:, :, :, :]).then_inc(v_hi_ready, 1)

            def conv_c(q, c):
                act.wait_ge(half_job, done(q, CONV + 2 * c, 0))
                copy(c_in, gemm[0][:, :]).then_inc(bank_free[0], 1)

            def conv_gate(q, c):
                act.wait_ge(half_job, done(q, CONV + 2 * c + 1, 1))
                nc.scalar.activation(c_gate, gemm[1][:, :], ACT.Sigmoid).then_inc(z_sig, 1)
                act.wait_ge(ua_mixed, q * KT + c + 1)
                copy(m_hi[:, c, :], c_y).then_inc(ua_hi_ready, 1)

            def quarter(q, last):
                with act.Fori(ZA, GATES) as pair:
                    for k in range(2):
                        act.wait_ge(half_job, done(q, pair, k))
                        nc.scalar.activation(silu_tmp[k], gemm[k][:, :], ACT.Sigmoid).then_inc(gate_sig, 1)

                def copy_gate(row, pair, k):
                    act.wait_ge(half_job, done(q, pair, k))
                    copy(gates[:, row, :], gemm[k][:, :]).then_inc(bank_free[k], 1)

                for s, k in slots():
                    if s == -1:
                        split_p(q, 0, 0)
                    exps(q, s + LEAD, k)
                    copy_gate(s + LEAD, GATES, k)

                def attention_step(i):
                    for g, pair, more_scores, more_transposes in steps(i):
                        u, k = GROUPS * i + g, g % 2
                        move_o(q, u)
                        if more_transposes:
                            split_p(q, u + 1, 1 - k)
                        if more_scores:
                            exps(q, u + LEAD, k)
                        ub_hi(q, u, i, g)
                        if more_scores:
                            copy_gate(u + LEAD, pair, k)
                        elif k == 0:
                            conv_c(q, 0)

                with act.Fori(0, TT - 1) as i:
                    attention_step(i)
                attention_step(TT - 1)
                conv_gate(q, 0)
                with act.Fori(1, KT) as c:
                    act.wait_ge(bank_free[1], freed(q, CONV + 2 * c - 1))
                    conv_c(q, c)
                    conv_gate(q, c)
                for first, row, evac in ((YA, 0, False), (YB, KT, True)):
                    if last:
                        with act.Fori(0, KT) as tile:
                            merge_sigmoid(row + tile)
                            if evac:
                                yb_hi(q, tile)
                    else:
                        with act.Fori(0, TT // 2) as i:
                            n = TT * (q + 1) + (first - YA) // 2 + i
                            for k in range(4):
                                merge_sigmoid(row + 4 * i + k)
                                if evac:
                                    yb_hi(q, 4 * i + k)
                                if k == 0:
                                    input_squares(n)
                                if k == 2:
                                    input_hi(n, (first - YA) // 2 + i, t_ps[:, :, :])
                with act.Fori(0, KT // 2) as i:
                    for k in range(2):
                        act.wait_ge(half_job, done(q, Y + i, k))
                        copy(za[:, 2 * i + k, :], gemm[k][:, :]).then_inc(bank_free[k], 1)
                if not last:
                    head(q + 1, q)
                else:
                    for t in range(TT):
                        squares_y(q * TT + t, (s_flat, t_flat)[t % 2], y_out[:, t, :], TT + t)
                    for t in range(TT):
                        store_y(q * TT + t, y_out[:, t, :])
                act.wait_ge(out_stored, (q + 1) * TT * 16)

            for t in range(TT):
                act.wait_ge(x_first_loaded[t], 16)
                nc.scalar.activation(y_out[:, t, :], x_first[:, t, :], ACT.Square, scale=D ** -0.5,
                                     accum_out=mean[:, t:t + 1]).then_inc(x_mean, 1)
            for t in range(TT):
                input_hi(t, t, (t_ps, s_tiles)[t % 2][:, :, :])
            head(0, None)
            with act.Fori(0, NQ - 1) as q:
                quarter(q, False)
            quarter(NQ - 1, True)

        @block.vector
        def _(dve):
            def mult(dst, a, b):
                return nc.vector.tensor_tensor(dst, a, b, ALU.mult)

            def minus(dst, a, b):
                return nc.vector.tensor_tensor(dst, a, b, ALU.subtract)

            def split_weights(loads, k):
                dve.wait_ge(w_loaded[k], 16 * loads)
                for half in range(2):
                    lo, hi = half * KT // 2, (half + 1) * KT // 2
                    nc.vector.tensor_copy(w_hi[k][:, lo:hi, :],
                                          w_raw[:, k, lo * P:hi * P].rearrange("p (c n) -> p c n", n=P))\
                        .then_inc(w_hi_ready, 1)

            def next_weights(q, pair, k):
                dve.wait_ge(half_job, done(q, pair, k))
                split_weights(freed(q, pair) + 1, k)

            def add_rope(q, pair, k, n):
                dve.wait_ge(rot_ready, q * ROPED + n + 1)
                mult(qr[k], gemm[k][:, :], rope[:, 0, :]).then_inc(bank_free[k], 1)

            def finish_rope(q, pair, k, n):
                dve.wait_ge(rot_scaled, q * ROPED + n + 1)
                dve.wait_ge(bank_free[k], freed(q, pair))
                nc.vector.tensor_add(qr[k], qr[k], rot[k]).then_inc(roped, 1)

            def q_lo(q, n, k, head):
                dve.wait_ge(rope_hi, q * ROPED + n + 1)
                minus(qu[HD:P, head, :], qr[k][0:HD, :], f32(qu[0:HD, head, :]))
                minus(qu[0:HD, head + 1, :], qr[k][HD:P, :], f32(qu[HD:P, head + 1, :])).then_inc(rope_lo, 1)

            def scale_scores(q, u, k, g):
                if not isinstance(u, int) or u >= 2:
                    dve.wait_ge(pt_ready, unit(q, u) - 2)
                dve.wait_ge(scores_ready, unit(q, u))
                nc.vector.memset(carrier[:, :], 0.0)
                for head in range(UNIT_HEADS):
                    n = UNIT_HEADS * g + head
                    ins = nc.vector.tensor_tensor_reduce(
                        out=prob[k][:, head, :], in0=s_ps[:, head, :], in1=mask[:, :, :].rearrange("p a k -> p (a k)"),
                        scale=HD ** -0.5, scalar=sink[:, n:n + 1], op0=ALU.add, op1=ALU.max,
                        accum_out=rowmax[:, k, head:head + 1])
                ins.then_inc(scores_used, 1)
                dve.wait_ge(scores_used, unit(q, u))
                minus(sinkd[:, k, :], sink[:, UNIT_HEADS * g:UNIT_HEADS * (g + 1)], rowmax[:, k, :])
                nc.vector.tensor_scalar(negmax[:, k, :], rowmax[:, k, :], -1.0, None, ALU.mult)\
                    .then_inc(negmax_ready, 1)

            def denominators(q, u, k):
                dve.wait_ge(exp_done, unit(q, u))
                nc.vector.tensor_add(denom[:, k, :], rowsum[:, k, :], sinkd[:, k, :]).then_inc(denom_ready, 1)
                dve.wait_ge(denom_ready, unit(q, u))
                nc.vector.reciprocal(rden[:, k, :], denom[:, k, :]).then_inc(rden_ready, 1)

            def split_p(q, u, k):
                dve.wait_ge(pt_hi_ready, unit(q, u))
                minus(pt_lo[k], t_flat.rearrange("p (a n) -> p a n", a=2), f32(pt_hi[k])).then_inc(pt_lo_ready, 1)

            def gate_o(q, u, b, g):
                dve.wait_ge(o_moved, unit(q, u))
                if g > 0:
                    dve.wait_ge(ub_ready, unit(q, u) - 1)
                nc.vector.tensor_add(att[0:HD, :, :], o_ps[0:HD, 0:UNIT_HEADS:2, :], otmp[0:HD, :, :])
                nc.vector.tensor_add(att[HD:P, :, :], o_ps[HD:P, 1:UNIT_HEADS:2, :], otmp[HD:P, :, :])\
                    .then_inc(o_added, 1)
                dve.wait_ge(o_added, unit(q, u))
                mult(att[:, :, :], att[:, :, :], za[:, 2 * g:2 * g + 2, bass.ds(b * P, P)]).then_inc(ub_gated, 1)

            def ub_lo(q, u, b, g):
                dve.wait_ge(ub_hi_ready, unit(q, u))
                row, cols = UNIT_HEADS * g, bass.ds(b * P, P)
                minus(qu[:, row + 1:row + UNIT_HEADS:2, cols], att[:, :, :], f32(qu[:, row:row + UNIT_HEADS:2, cols]))\
                    .then_inc(ub_ready, 1)

            def norm_input(n, src, column):
                dve.wait_ge(x_rstd, n + 1)
                nc.vector.scalar_tensor_tensor(src, src, rstd[:, column:column + 1], gpre[:, :], ALU.mult, ALU.mult)\
                    .then_inc(x_normed, 1)

            def input_lo(n, t, src):
                dve.wait_ge(h_hi_ready, n + 1)
                minus(h_lo[:, :, bass.ds(t * P, P)], src, f32(h_hi[:, :, bass.ds(t * P, P)])).then_inc(h_ready, 1)

            def merge_a(q, pair, k, tile):
                next_weights(q, pair, k)
                dve.wait_ge(merge_sig, 2 * KT * q + tile + 1)
                mult(ga[:, tile, :], gemm[k][:, :], ga[:, tile, :]).then_inc(bank_free[k], 1)

            def merge_b(q, pair, k, tile):
                next_weights(q, pair, k)
                dve.wait_ge(merge_sig, 2 * KT * q + KT + tile + 1)
                mult(gb[:, tile, :], gemm[k][:, :], gb[:, tile, :]).then_inc(bank_free[k], 1)
                dve.wait_ge(bank_free[k], freed(q, pair))
                nc.vector.tensor_add(gb[:, tile, :], gb[:, tile, :], ga[:, tile, :]).then_inc(merged, 1)
                dve.wait_ge(m_hi_ready, q * KT + tile + 1)
                minus(m_lo[:, tile, :], gb[:, tile, :], f32(m_hi[:, tile, :])).then_inc(m_ready, 1)

            def finish_y(n, t, src, column, scaled, total):
                dve.wait_ge(y_rstd, n + 1)
                nc.vector.scalar_tensor_tensor(scaled, src, rstd[:, column:column + 1], gpost, ALU.mult, ALU.mult)\
                    .then_inc(y_scaled, 1)
                dve.wait_ge(y_scaled, n + 1)
                nc.vector.tensor_add(total, scaled, x_last[:, t, :]).then_inc(y_summed, 1)

            def head(q, before):
                nc.vector.tensor_copy(kk[:, :, :, 0:P], f32(kk[:, :, :, T:T + P]))
                nc.vector.tensor_copy(vv[:, 0, :, :], f32(vv[:, TT, :, :])).then_inc(kv_carried, 1)
                next_weights(q, KV, 0)
                dve.wait_ge(rope_loaded, 16 * (q + 1))
                add_rope(q, KV, 0, 0)
                finish_rope(q, KV, 0, 0)
                next_weights(q, KV, 1)
                dve.wait_ge(rope_hi, q * ROPED + 1)
                for g in range(KVH):
                    own = slice(HD * g, HD * (g + 1))
                    for half in range(2):
                        ins = minus(kk[HD * half:HD * (half + 1), g, 1, P:P + T], qr[0][own, :],
                                    f32(kk[own, g, 0, P:P + T]))
                ins.then_inc(rope_lo, 1)
                with dve.Fori(0, TT) as i:
                    next_weights(q, Q + i, 0)
                    dve.wait_ge(rope_lo, q * ROPED + 1 + 2 * i)
                    add_rope(q, Q + i, 0, 1 + 2 * i)
                    finish_rope(q, Q + i, 0, 1 + 2 * i)
                    if before is not None:
                        dve.wait_ge(tail_loaded, 32 * (before + 1))
                        finish_y(before * TT + i, i, t_flat, TT, y_scaled_row, x_last[:, i, :])
                    q_lo(q, 1 + 2 * i, 0, 4 * i)
                    next_weights(q, Q + i, 1)
                    add_rope(q, Q + i, 1, 2 + 2 * i)
                    finish_rope(q, Q + i, 1, 2 + 2 * i)
                    q_lo(q, 2 + 2 * i, 1, 4 * i + 2)
                dve.wait_ge(v_hi_ready, q + 1)
                minus(vv[:, 1:1 + TT, :, HD:2 * HD], v_ps[:, :, :, :], f32(vv[:, 1:1 + TT, :, 0:HD]))\
                    .then_inc(v_ready, 1)

            def conv_taps(q, c):
                pair, tap = CONV + 2 * c, 3 * (q * KT + c)
                nc.vector.tensor_copy(c_u[:, 0:2], halo[:, c, :]).then_inc(halo_in, 1)
                dve.wait_ge(bank_free[0], freed(q, pair))
                mult(c_u[:, 2:T + 2], gemm[1][:, :], c_in).then_inc(bank_free[1], 1)
                dve.wait_ge(halo_in, q * KT + c + 1)
                dve.wait_ge(bank_free[1], freed(q, pair))
                nc.vector.tensor_scalar(c_y, c_u[:, 0:T], taps[:, c, 0:1], None, ALU.mult).then_inc(tap_done, 1)
                nc.vector.tensor_copy(halo[:, c, :], c_u[:, T:T + 2])
                dve.wait_ge(tap_done, tap + 1)
                nc.vector.scalar_tensor_tensor(c_y, c_u[:, 1:T + 1], taps[:, c, 1:2], c_y, ALU.mult, ALU.add)\
                    .then_inc(tap_done, 1)
                dve.wait_ge(tap_done, tap + 2)
                nc.vector.scalar_tensor_tensor(c_y, c_u[:, 2:T + 2], taps[:, c, 2:3], c_y, ALU.mult, ALU.add)\
                    .then_inc(tap_done, 1)

            def conv_gate(q, c):
                pair = CONV + 2 * c + 1
                next_weights(q, pair, 0)
                dve.wait_ge(tap_done, 3 * (q * KT + c) + 3)
                mult(c_y, gemm[0][:, :], c_y).then_inc(bank_free[0], 1)
                next_weights(q, pair, 1)
                dve.wait_ge(z_sig, q * KT + c + 1)
                mult(c_gate, gemm[1][:, :], c_gate).then_inc(bank_free[1], 1)
                dve.wait_ge(bank_free[1], freed(q, pair))
                mult(c_y, c_y, c_gate).then_inc(ua_mixed, 1)
                dve.wait_ge(ua_hi_ready, q * KT + c + 1)
                minus(m_lo[:, c, :], c_y, f32(m_hi[:, c, :])).then_inc(ua_ready, 1)

            def quarter(q, last):
                with dve.Fori(0, KT // 2) as i:
                    for k in range(2):
                        next_weights(q, ZA + i, k)
                        dve.wait_ge(gate_sig, q * KT + 2 * i + k + 1)
                        mult(za[:, 2 * i + k, :], gemm[k][:, :], silu_tmp[k]).then_inc(bank_free[k], 1)

                for s, k in slots():
                    scale_scores(q, s + LEAD, k, s + LEAD)
                    if s == -1:
                        split_p(q, 0, 0)
                    denominators(q, s + LEAD, k)
                    next_weights(q, GATES, k)

                def attention_step(i):
                    for g, pair, more_scores, more_transposes in steps(i):
                        u, k = GROUPS * i + g, g % 2
                        if more_scores:
                            scale_scores(q, u + LEAD, k, (g + LEAD) % GROUPS)
                            if g + LEAD == GROUPS - 1:
                                nc.vector.tensor_copy(mask[:, 0, :], band[:, 0, :]).then_inc(mask_full, 1)
                        gate_o(q, u, i, g)
                        if more_transposes:
                            split_p(q, u + 1, 1 - k)
                        if more_scores:
                            denominators(q, u + LEAD, k)
                        ub_lo(q, u, i, g)
                        next_weights(q, pair, k)

                with dve.Fori(0, TT - 1) as i:
                    attention_step(i)
                attention_step(TT - 1)

                conv_taps(q, 0)
                conv_gate(q, 0)
                with dve.Fori(1, KT) as c:
                    for k in range(2):
                        next_weights(q, CONV + 2 * c, k)
                    conv_taps(q, c)
                    conv_gate(q, c)
                for first, merge in ((YA, merge_a), (YB, merge_b)):
                    if last:
                        with dve.Fori(0, KT // 2) as i:
                            for k in range(2):
                                merge(q, first + i, k, 2 * i + k)
                    else:
                        with dve.Fori(0, TT // 2) as i:
                            n = TT * (q + 1) + (first - YA) // 2 + i
                            for k in range(4):
                                if k == 2:
                                    norm_input(n, xs, 0)
                                if k == 3:
                                    input_lo(n, (first - YA) // 2 + i, t_ps[:, :, :])
                                merge(q, first + 2 * i + k // 2, k % 2, 4 * i + k)
                if last:
                    with dve.Fori(Y, PAIRS - 1) as pair:
                        for k in range(2):
                            next_weights(q, pair, k)
                else:
                    with dve.Fori(Y, PAIRS) as pair:
                        for k in range(2):
                            next_weights(q, pair, k)
                if not last:
                    head(q + 1, q)
                    return
                dve.wait_ge(tail_loaded, 32 * (q + 1))
                for t in range(TT):
                    finish_y(q * TT + t, t, (s_flat, t_flat)[t % 2], TT + t, y_out[:, t, :], y_out[:, t, :])

            nc.vector.memset(halo[:, :, :], 0.0)
            for k in range(2):
                split_weights(1, k)
            nc.vector.memset(kk[:, :, :, :].bitcast(F32), 0.0)
            nc.vector.memset(vv[:, :, :, :].bitcast(F32), 0.0).then_inc(kv_zeroed, 1)
            dve.wait_ge(gain_loaded, 2 * 16)
            for t in range(TT):
                norm_input(t, x_first[:, t, :], t)
            for t in range(TT):
                input_lo(t, t, (t_ps, s_tiles)[t % 2][:, :, :])
            dve.wait_ge(kv_zeroed, 1)
            dve.wait_ge(consts_loaded, N_CONSTS)
            head(0, None)
            with dve.Fori(0, NQ - 1) as q:
                quarter(q, False)
            quarter(NQ - 1, True)

        @block.gpsimd
        def _(pool):
            def split_weights(before, k):
                for half in range(2):
                    lo, hi = half * KT // 2, (half + 1) * KT // 2
                    pool.wait_ge(w_hi_ready, before + half + 1)
                    nc.gpsimd.tensor_tensor(w_lo[k][:, lo:hi, :],
                                            w_raw[:, k, lo * P:hi * P].rearrange("p (c n) -> p c n", n=P),
                                            f32(w_hi[k][:, lo:hi, :]), ALU.subtract).then_inc(w_lo_ready, 1)

            def next_weights(q, pair, k):
                split_weights(done(q, pair, k) + 2, k)

            def next_pairs(q, first, end):
                with pool.Fori(first, end) as pair:
                    for k in range(2):
                        next_weights(q, pair, k)

            def scale_rot(q, n, k):
                pool.wait_ge(rot_ready, q * ROPED + n + 1)
                nc.gpsimd.tensor_tensor(rot[k], rot[k], rope[:, 1, :], ALU.mult).then_inc(rot_scaled, 1)

            def normalise(q, u, k):
                pool.wait_ge(rden_ready, unit(q, u))
                nc.gpsimd.tensor_tensor(prob[k], prob[k],
                                        rden[:, k, :].unsqueeze(2).broadcast_to([P, UNIT_HEADS, 2 * P]),
                                        ALU.mult).then_inc(probs_ready, 1)

            def inverse_root(column, n, mean_sem, msq_sem, rstd_sem):
                cols = slice(column, column + 1)
                pool.wait_ge(mean_sem, n + 1)
                nc.gpsimd.tensor_tensor(msq[:, cols], mean[:, cols], root_consts[:, 1:2], ALU.add).then_inc(msq_sem, 1)
                pool.wait_ge(msq_sem, n + 1)
                nc.gpsimd.tensor_tensor(rstd[:, cols], msq[:, cols], root_consts[:, 0:1], ALU.pow).then_inc(rstd_sem, 1)

            def head(q, before):
                next_weights(q, KV, 0)
                pool.wait_ge(rope_loaded, 16 * (q + 1))
                scale_rot(q, 0, 0)
                next_weights(q, KV, 1)
                with pool.Fori(0, TT) as i:
                    next_weights(q, Q + i, 0)
                    scale_rot(q, 1 + 2 * i, 0)
                    if before is not None:
                        inverse_root(TT, before * TT + i, y_mean, y_msq, y_rstd)
                    next_weights(q, Q + i, 1)
                    scale_rot(q, 2 + 2 * i, 1)

            def quarter(q, last):
                next_pairs(q, ZA, GATES)
                for s, k in slots():
                    normalise(q, s + LEAD, k)
                    next_weights(q, GATES, k)

                def attention_step(i):
                    for g, pair, more_scores, _ in steps(i):
                        if more_scores:
                            normalise(q, GROUPS * i + g + LEAD, g % 2)
                        next_weights(q, pair, g % 2)

                with pool.Fori(0, TT - 1) as i:
                    attention_step(i)
                attention_step(TT - 1)
                next_pairs(q, CONV + 1, YA)
                if last:
                    next_pairs(q, YA, PAIRS - 1)
                else:
                    with pool.Fori(0, TT) as t:
                        next_weights(q, YA + 2 * t, 0)
                        inverse_root(0, TT * (q + 1) + t, x_mean, x_msq, x_rstd)
                        next_weights(q, YA + 2 * t, 1)
                        next_weights(q, YA + 2 * t + 1, 0)
                        next_weights(q, YA + 2 * t + 1, 1)
                    next_pairs(q, Y, PAIRS)
                    head(q + 1, q)
                    return
                for t in range(TT):
                    inverse_root(TT + t, q * TT + t, y_mean, y_msq, y_rstd)

            nc.gpsimd.memset(root_consts[:, 0:1], -0.5)
            nc.gpsimd.memset(root_consts[:, 1:2], EPS).then_inc(root_consts_set, 1)
            pool.wait_ge(root_consts_set, 1)
            for t in range(TT):
                inverse_root(t, t, x_mean, x_msq, x_rstd)
            for k in range(2):
                split_weights(2 * k, k)
            head(0, None)
            with pool.Fori(0, NQ - 1) as q:
                quarter(q, False)
            quarter(NQ - 1, True)


def weight_tiles(w_in, w_proj_conv, w_proj_attn, w_out):
    widths = (D, D, D, D, D, KVH * HD, KVH * HD, D, D, D)
    ends = np.cumsum(widths)
    xc, bg, cg, zc, q, k, v, za, ga, gb = (w_in[:, e - w:e] for e, w in zip(ends, widths))
    cols = [k, v, q, za, ga, gb]
    for c in range(KT):
        cols += [m[:, c * P:(c + 1) * P] for m in (cg, xc, bg, zc)]
    cols += [w_proj_conv, w_proj_attn, w_out]
    w = np.concatenate(cols, axis=1)
    return np.ascontiguousarray(w.reshape(KT, P, JOBS, P).transpose(2, 1, 0, 3).reshape(JOBS, P, D))


def rope_tables():
    inv = (10000.0 ** (-np.arange(0, HD, 2, dtype=np.float32) / np.float32(HD))).astype(np.float32)
    angle = (np.arange(SEQ, dtype=np.float32)[:, None] * inv[None, :]).astype(np.float32).astype(np.float64)
    cos, sin = np.cos(angle).T, np.sin(angle).T
    both = np.stack([np.concatenate([cos] * 4), np.concatenate([-sin, sin] * 2)], axis=1)
    return np.ascontiguousarray(both.reshape(P, 2, NQ, T).transpose(2, 0, 1, 3).reshape(NQ, P, 2 * T).astype(np.float32))


def mask_table():
    qi, kj = np.arange(P)[:, None], np.arange(P)[None, :]
    previous = np.where(kj > qi, 0.0, MASKED)
    own = np.where(kj <= qi, 0.0, MASKED)
    return np.concatenate([np.eye(P), previous, own, np.full((P, P), MASKED), own], axis=1).astype(np.float32)


def kernel(x, g_pre, g_post, w_in, w_conv, sinks, w_proj_conv, w_proj_attn, w_out):
    import concourse.bacc as bacc
    from concourse.bass_utils import run_bass_kernel_spmd

    arrays = {
        "x": np.ascontiguousarray(np.asarray(x)[0]),
        "wjobs": weight_tiles(*(np.asarray(w)[0] for w in (w_in, w_proj_conv, w_proj_attn, w_out))),
        "g_pre": np.ascontiguousarray(np.asarray(g_pre)),
        "g_post": np.ascontiguousarray(np.asarray(g_post)),
        "w_conv": np.ascontiguousarray(np.asarray(w_conv)[0].reshape(3, KT, P).transpose(2, 1, 0)),
        "sinks": np.ascontiguousarray(np.asarray(sinks)),
        "tables": rope_tables(),
        "masks": mask_table(),
    }
    nc = bacc.Bacc("TRN2", target_bir_lowering=False, num_devices=1)
    args = [nc.dram_tensor(name, a.shape, F32, kind="ExternalInput").ap() for name, a in arrays.items()]
    out = nc.dram_tensor("out", (SEQ, D), F32, kind="ExternalOutput").ap()
    build(nc, *args, out)
    result = run_bass_kernel_spmd(nc, [arrays], core_ids=[0])
    return result.results[0]["out"].reshape(1, SEQ, D)
```

```python
from contextlib import ExitStack

import numpy as np

import concourse.bass as bass
from concourse import mybir

F32 = mybir.dt.float32
F32R = mybir.dt.float32r
ACT = mybir.ActivationFunctionType
ALU = mybir.AluOpType

P = 128
SEQ, D = 2048, 1024
KT = D // P
T = 512
NQ = SEQ // T
TT = T // P
HEADS, HD, KVH = 16, 64, 2
UNIT_HEADS = 4
GROUPS = HEADS // UNIT_HEADS
UNITS = TT * GROUPS
EPS = 1e-6
MASKED = -1e30

KV, Q, ZA, GATES, CONV, YA, YB, Y, PAIRS = 0, 1, 5, 9, 17, 33, 37, 41, 45
JOBS = 2 * PAIRS
LEAD = 2
ROPED = 1 + HEADS // 2


def build(nc, x, wjobs, g_pre, g_post, w_conv, sinks, tables, masks, out):
    ctx = ExitStack()
    with ctx:
        def sbuf(name, shape, dtype=F32):
            return ctx.enter_context(nc.sbuf_tensor(name, shape, dtype))

        def psum(name, shape):
            return ctx.enter_context(nc.psum_tensor(name, shape, F32))

        def sem(name):
            return ctx.enter_context(nc.semaphore(name))

        h_hi = sbuf("h_hi", [P, KT, T], F32R)
        h_lo = sbuf("h_lo", [P, KT, T], F32R)
        qu = sbuf("qu", [P, HEADS, T], F32R)
        m_hi = sbuf("m_hi", [P, KT, T], F32R)
        m_lo = sbuf("m_lo", [P, KT, T], F32R)
        za = sbuf("za", [P, KT, T])
        gates = sbuf("gates", [P, 2 * KT, T])
        ga, gb = gates[:, 0:KT, :], gates[:, KT:2 * KT, :]
        w_raw = sbuf("w_raw", [P, 2, D])
        w_hi = [sbuf(f"w_hi{i}", [P, KT, P], F32R) for i in range(2)]
        w_lo = [sbuf(f"w_lo{i}", [P, KT, P], F32R) for i in range(2)]
        kk = sbuf("kk", [P, KVH, 2, P + T], F32R)
        vv = sbuf("vv", [P, 1 + TT, KVH, 2 * HD], F32R)
        rope = sbuf("rope", [P, 2, T])
        band = sbuf("band", [P, 2, P])
        mask = sbuf("mask", [P, 2, P])
        ident = sbuf("ident", [P, P])
        gpre = sbuf("gpre", [P, D])
        taps = sbuf("taps", [P, KT, 3])
        sink = sbuf("sink", [P, HEADS])
        halo = sbuf("halo", [P, KT, 2])
        otmp = sbuf("otmp", [P, 2, P])
        att = sbuf("att", [P, 2, P])
        rowmax = sbuf("rowmax", [P, 2, UNIT_HEADS])
        negmax = sbuf("negmax", [P, 2, UNIT_HEADS])
        sinkd = sbuf("sinkd", [P, 2, UNIT_HEADS])
        rowsum = sbuf("rowsum", [P, 2, UNIT_HEADS])
        denom = sbuf("denom", [P, 2, UNIT_HEADS])
        rden = sbuf("rden", [P, 2, UNIT_HEADS])
        mean = sbuf("mean", [P, 2 * TT])
        msq = sbuf("msq", [P, 2 * TT])
        rstd = sbuf("rstd", [P, 2 * TT])
        root_consts = sbuf("root_consts", [P, 2])
        carrier = sbuf("carrier", [P, 1])
        work = sbuf("work", [P, 4 * T + 2])

        def f32(ap):
            return ap.bitcast(F32)

        prob = [work[:, i * 2 * T:(i + 1) * 2 * T].rearrange("p (h k) -> p h k", h=UNIT_HEADS)
                for i in range(2)]
        c_in, c_y, c_gate = (work[:, i * T:(i + 1) * T] for i in range(3))
        c_u = work[:, 3 * T:4 * T + 2]
        xs = gpost = work[:, 0:D]
        v_raw = gb[:, 0, :]
        rot = [gb[:, 1 + i, :] for i in range(2)]
        qr = [gb[:, (3, 6)[i], :] for i in range(2)]
        silu_tmp = [gb[:, 4 + i, :] for i in range(2)]

        def token_rows(tensor):
            return tensor.rearrange("p (t a) n -> p t (a n)", t=TT)

        x_first, x_last, y_out = token_rows(za[:, :, :]), token_rows(ga), token_rows(gb)
        y_squares = m_lo[:, 0:2, :].rearrange("p a n -> p (a n)")
        y_scaled_row = work[:, D:2 * D]
        pt_hi = [m_hi[:, 2 * i:2 * i + 2, :] for i in range(2)]
        pt_lo = [m_lo[:, 2 * i:2 * i + 2, :] for i in range(2)]

        gemm_ps = psum("gemm_ps", [P, 2, T])
        gemm = [gemm_ps[:, k, :] for k in range(2)]
        s_ps = psum("s_ps", [P, UNIT_HEADS, 2 * P])
        t_ps = psum("t_ps", [P, KT, P])
        ov_ps = psum("ov_ps", [P, 2, T])
        o_flat = ov_ps[:, 0, :]
        o_ps = o_flat.rearrange("p (h t) -> p h t", h=UNIT_HEADS)
        v_ps = ov_ps[:, 1, :].rearrange("p (b g d) -> p b g d", b=TT, g=KVH)
        s_flat = s_ps[:, :, :].rearrange("p h k -> p (h k)")
        t_flat = t_ps[:, :, :].rearrange("p h k -> p (h k)")
        row_flat = [s_flat, t_flat] + [ps[:, :, :].rearrange("p k t -> p (k t)") for ps in (ov_ps, gemm_ps)]
        row_tiles = [flat.rearrange("p (c n) -> p c n", n=P) for flat in row_flat]

        gain_loaded = sem("gain_loaded")
        consts_loaded = sem("consts_loaded")
        kv_zeroed = sem("kv_zeroed")
        root_consts_set = sem("root_consts_set")
        w_loaded = [sem(f"w_loaded{i}") for i in range(2)]
        w_hi_ready = sem("w_hi_ready")
        w_lo_ready = sem("w_lo_ready")
        half_job = sem("half_job")
        bank_free = [sem(f"bank_free{i}") for i in range(2)]
        x_first_loaded = [sem(f"x_first_loaded{t}") for t in range(TT)]
        xs_loaded = sem("xs_loaded")
        x_mean = sem("x_mean")
        x_msq = sem("x_msq")
        x_rstd = sem("x_rstd")
        x_normed = sem("x_normed")
        h_transposed = sem("h_transposed")
        h_hi_ready = sem("h_hi_ready")
        h_ready = sem("h_ready")
        rope_loaded = sem("rope_loaded")
        kv_carried = sem("kv_carried")
        rot_ready = sem("rot_ready")
        rot_scaled = sem("rot_scaled")
        roped = sem("roped")
        rope_hi = sem("rope_hi")
        rope_lo = sem("rope_lo")
        v_transposed = sem("v_transposed")
        v_hi_ready = sem("v_hi_ready")
        v_ready = sem("v_ready")
        gate_sig = sem("gate_sig")
        scores_ready = sem("scores_ready")
        scores_used = sem("scores_used")
        mask_full = sem("mask_full")
        negmax_ready = sem("negmax_ready")
        exp_done = sem("exp_done")
        denom_ready = sem("denom_ready")
        rden_ready = sem("rden_ready")
        probs_ready = sem("probs_ready")
        pt_ready = sem("pt_ready")
        pt_hi_ready = sem("pt_hi_ready")
        pt_lo_ready = sem("pt_lo_ready")
        o_ready = sem("o_ready")
        o_moved = sem("o_moved")
        o_added = sem("o_added")
        ub_gated = sem("ub_gated")
        ub_hi_ready = sem("ub_hi_ready")
        ub_ready = sem("ub_ready")
        halo_in = sem("halo_in")
        tap_done = sem("tap_done")
        z_sig = sem("z_sig")
        ua_mixed = sem("ua_mixed")
        ua_hi_ready = sem("ua_hi_ready")
        ua_ready = sem("ua_ready")
        merge_sig = sem("merge_sig")
        merged = sem("merged")
        m_hi_ready = sem("m_hi_ready")
        m_ready = sem("m_ready")
        tail_loaded = sem("tail_loaded")
        y_transposed = sem("y_transposed")
        y_mean = sem("y_mean")
        y_msq = sem("y_msq")
        y_rstd = sem("y_rstd")
        y_scaled = sem("y_scaled")
        y_summed = sem("y_summed")
        y_added = sem("y_added")
        out_stored = sem("out_stored")
        N_CONSTS = 4 * 16

        def done(q, pair, k):
            return q * 2 * JOBS + pair * 4 + 2 * k + 2

        def freed(q, pair):
            return q * PAIRS + pair + 1

        def unit(q, u):
            return q * UNITS + u + 1

        def steps(i):
            last = isinstance(i, int)
            for g in range(GROUPS):
                yield (g, GATES + 2 * i + (g + LEAD) // 2, not (last and g + LEAD >= GROUPS),
                       not (last and g + 1 >= GROUPS))

        block = ctx.enter_context(nc.Block())

        @block.sync
        def _(sp):
            for t in range(TT):
                sp.dma_start(x_first[:, t, :], x[t * P:(t + 1) * P, :]).then_inc(x_first_loaded[t], 16)
                if t == 0:
                    sp.dma_start(gpre[:, :], g_pre.broadcast_to([P, D])).then_inc(gain_loaded, 16)
                    sp.dma_start(ident[:, :], masks[:, 0:P]).then_inc(gain_loaded, 16)
            for k in range(2):
                sp.dma_start(w_raw[:, k, :], wjobs[k]).then_inc(w_loaded[k], 16)
            sp.dma_start(band[:, :, :], masks[:, P:3 * P].rearrange("p (a k) -> p a k", a=2)).then_inc(consts_loaded, 16)
            sp.dma_start(mask[:, :, :], masks[:, 3 * P:5 * P].rearrange("p (a k) -> p a k", a=2)).then_inc(consts_loaded, 16)
            sp.dma_start(taps[:, :, :], w_conv).then_inc(consts_loaded, 16)
            sp.dma_start(sink[:, :], sinks.broadcast_to([P, HEADS])).then_inc(consts_loaded, 16)

            def load_pair(q, pair, nxt):
                for k in range(2):
                    sp.wait_ge(w_lo_ready, done(q, pair, k))
                    sp.dma_start(w_raw[:, k, :], wjobs[2 * nxt + k]).then_inc(w_loaded[k], 16)

            def loads(q, first, end):
                with sp.Fori(first, end) as pair:
                    load_pair(q, pair, pair + 1)

            def load_rope(q):
                sp.dma_start(rope[:, :, :], tables[q].rearrange("p (a t) -> p a t", a=2)).then_inc(rope_loaded, 16)

            def quarter(q, last):
                loads(q, 0, YA)
                if not last:
                    sp.wait_ge(roped, (q + 1) * ROPED)
                    load_rope(q + 1)
                if last:
                    loads(q, YA, Y + 1)
                else:
                    with sp.Fori(0, TT) as t:
                        load_pair(q, YA + 2 * t, YA + 2 * t + 1)
                        sp.wait_ge(ua_ready, KT * (q + 1))
                        sp.wait_ge(h_transposed, TT * (q + 1) + t)
                        sp.dma_start(xs, x[bass.ds((q + 1) * T + t * P, P), :]).then_inc(xs_loaded, 16)
                        load_pair(q, YA + 2 * t + 1, YA + 2 * t + 2)
                    load_pair(q, Y, Y + 1)
                sp.wait_ge(m_ready, KT * (q + 1))
                if not last:
                    sp.wait_ge(h_transposed, TT * (q + 2))
                sp.dma_start(x_last, x[bass.ds(q * T, T), :].rearrange("(t p) d -> p t d", p=P)).then_inc(tail_loaded, 16)
                sp.dma_start(gpost, g_post.broadcast_to([P, D])).then_inc(tail_loaded, 16)
                loads(q, Y + 1, PAIRS - 1)
                if not last:
                    load_pair(q, PAIRS - 1, 0)

            load_rope(0)
            with sp.Fori(0, NQ - 1) as q:
                quarter(q, False)
            quarter(NQ - 1, True)

        @block.tensor
        def _(pe):
            def job(q, pair, k, hi, lo, tiles=None, per_quarter=KT, first=False):
                if tiles is not None:
                    pe.wait_ge(tiles, per_quarter * (q + 1) - 1)
                if not first:
                    pe.wait_ge(bank_free[k], freed(q, pair) - 1)
                for kt in range(KT):
                    if kt % (KT // 2) == 0:
                        pe.wait_ge(w_lo_ready, done(q, pair, k) - 1 + kt // (KT // 2))
                    if kt == KT - 1 and tiles is not None:
                        pe.wait_ge(tiles, per_quarter * (q + 1))
                    for n, (w, moving) in enumerate(((w_lo[k], hi), (w_hi[k], lo), (w_hi[k], hi))):
                        ins = nc.tensor.matmul(gemm[k][:, :], w[:, kt, :], moving[:, kt, :],
                                               start=kt == 0 and n == 0, stop=kt == KT - 1 and n == 2)
                    if kt % (KT // 2) == KT // 2 - 1:
                        ins.then_inc(half_job, 1)

            def jobs(q, first, end, *operand):
                with pe.Fori(first, end) as pair:
                    for k in range(2):
                        job(q, pair, k, *operand)

            h, m = (h_hi, h_lo), (m_hi, m_lo)
            ub = (qu[:, 0:HEADS:2, :], qu[:, 1:HEADS:2, :])

            def transpose_h(ready, src, dst, read=0):
                pe.wait_ge(x_normed, ready)
                if read:
                    pe.wait_ge(h_ready, read)
                for c in range(KT):
                    ins = nc.tensor.transpose(dst[:, c, :], src[:, c * P:(c + 1) * P], ident[:, :])
                ins.then_inc(h_transposed, 1)

            def scores(q, u):
                b, g = divmod(u, GROUPS)
                if u == 0:
                    pe.wait_ge(rope_lo, (q + 1) * ROPED)
                if u > 0:
                    pe.wait_ge(scores_used, unit(q, u) - 1)
                for head in range(UNIT_HEADS):
                    for part in (1, 0):
                        ins = nc.tensor.matmul(s_ps[:, head, :], qu[:, UNIT_HEADS * g + head, b * P:(b + 1) * P],
                                               kk[:, g // 2, part, b * P:(b + 2) * P], start=part == 1, stop=part == 0)
                ins.then_inc(scores_ready, 1)

            def transpose_p(q, u):
                pe.wait_ge(probs_ready, unit(q, u))
                for part in range(2):
                    for head in range(UNIT_HEADS):
                        ins = nc.tensor.transpose(t_ps[:, UNIT_HEADS * part + head, :],
                                                  prob[u % 2][:, head, part * P:(part + 1) * P], ident[:, :])
                ins.then_inc(pt_ready, 1)

            def values(q, u):
                b, g = divmod(u, GROUPS)
                pe.wait_ge(pt_lo_ready, unit(q, u))
                if u > 0:
                    pe.wait_ge(o_added, unit(q, u) - 1)
                if u == 0:
                    pe.wait_ge(v_ready, q + 1)
                for n in range(4):
                    part, pt = n // 2, (pt_lo, pt_hi)[n % 2][u % 2]
                    ins = nc.tensor.matmul(o_flat, vv[:, b + part, g // 2, :],
                                           pt[:, part, :], start=n == 0, stop=n == 3)
                ins.then_inc(o_ready, 1)

            def transpose_y(n, t, dst):
                for c in range(KT):
                    ins = nc.tensor.transpose(dst[:, c, :], za[:, c, t * P:(t + 1) * P], ident[:, :])
                ins.then_inc(y_transposed, 1)

            def head(q, before):
                pe.wait_ge(h_ready, TT * (q + 1))
                for k in range(2):
                    job(q, KV, k, *h, first=before is None)
                if before is None:
                    jobs(q, Q, ZA, *h)
                else:
                    for t in range(TT):
                        job(q, Q + t, 0, *h)
                        if t > 0:
                            pe.wait_ge(y_scaled, before * TT + t)
                        transpose_y(before * TT + t, t, t_ps)
                        job(q, Q + t, 1, *h)
                pe.wait_ge(bank_free[1], freed(q, KV))
                for b in range(TT):
                    ins = nc.tensor.transpose(v_ps[:, b, :, :].rearrange("p g d -> p (g d)"),
                                              v_raw[:, b * P:(b + 1) * P], ident[:, :])
                ins.then_inc(v_transposed, 1)
                for k in range(2):
                    job(q, ZA, k, *h)

            def quarter(q, last):
                jobs(q, ZA + 1, GATES - 1, *h)
                job(q, GATES - 1, 0, *h)
                scores(q, 0)
                job(q, GATES - 1, 1, *h)
                for s in range(-LEAD, UNITS):
                    if 0 < s + LEAD < UNITS:
                        scores(q, s + LEAD)
                    if s >= 0:
                        values(q, s)
                    if 0 <= s + 1 < UNITS:
                        transpose_p(q, s + 1)
                    job(q, GATES + (s + LEAD) // 2, s % 2, *h)
                jobs(q, CONV + 1, YA, *h)
                for first, operand in ((YA, (*m, ua_ready)), (YB, (*ub, ub_ready, UNITS))):
                    if last:
                        jobs(q, first, first + KT // 2, *operand)
                    else:
                        with pe.Fori(0, TT // 2) as i:
                            job(q, first + 2 * i, 0, *operand)
                            job(q, first + 2 * i, 1, *operand)
                            job(q, first + 2 * i + 1, 0, *operand)
                            transpose_h(TT * (q + 1) + (first - YA) // 2 + i + 1, xs, t_ps)
                            job(q, first + 2 * i + 1, 1, *operand)
                jobs(q, Y, PAIRS, *m, m_ready)
                if not last:
                    head(q + 1, q)
                    return
                for k in range(2):
                    pe.wait_ge(bank_free[k], freed(q, PAIRS - 1))
                for t in range(TT):
                    transpose_y(q * TT + t, t, row_tiles[t])

            pe.wait_ge(gain_loaded, 2 * 16)
            for t in range(TT):
                transpose_h(t + 1, x_first[:, t, :], row_tiles[t])
            head(0, None)
            with pe.Fori(0, NQ - 1) as q:
                quarter(q, False)
            quarter(NQ - 1, True)

        @block.scalar
        def _(act):
            def copy(dst, src):
                return nc.scalar.activation(dst, src, ACT.Copy)

            def rotate(q, pair, k):
                act.wait_ge(half_job, done(q, pair, k))
                for a in range(4):
                    b = a ^ 1
                    ins = copy(rot[k][32 * b:32 * b + 32, :], gemm[k][32 * a:32 * a + 32, :])
                ins.then_inc(rot_ready, 1)

            def q_hi(q, n, k, head):
                act.wait_ge(roped, q * ROPED + n + 1)
                copy(qu[0:HD, head, :], qr[k][0:HD, :])
                copy(qu[HD:P, head + 1, :], qr[k][HD:P, :]).then_inc(rope_hi, 1)

            def exps(q, u, k):
                act.wait_ge(negmax_ready, unit(q, u))
                for head in range(UNIT_HEADS):
                    nc.scalar.activation(prob[k][:, head, :], prob[k][:, head, :], ACT.Exp,
                                         bias=negmax[:, k, head:head + 1], accum_out=rowsum[:, k, head:head + 1])
                nc.scalar.activation(sinkd[:, k, :], sinkd[:, k, :], ACT.Exp).then_inc(exp_done, 1)

            def split_p(q, u, k):
                act.wait_ge(pt_ready, unit(q, u))
                copy(pt_hi[k], t_flat.rearrange("p (a n) -> p a n", a=2)).then_inc(pt_hi_ready, 1)

            def move_o(q, u):
                act.wait_ge(o_ready, unit(q, u))
                copy(otmp[0:HD, :, :], o_ps[HD:P, 0:UNIT_HEADS:2, :])
                copy(otmp[HD:P, :, :], o_ps[0:HD, 1:UNIT_HEADS:2, :]).then_inc(o_moved, 1)

            def ub_hi(q, u, b, g):
                act.wait_ge(ub_gated, unit(q, u))
                copy(qu[:, UNIT_HEADS * g:UNIT_HEADS * (g + 1):2, bass.ds(b * P, P)], att[:, :, :])\
                    .then_inc(ub_hi_ready, 1)

            def merge_sigmoid(row):
                nc.scalar.activation(gates[:, row, :], gates[:, row, :], ACT.Sigmoid).then_inc(merge_sig, 1)

            def yb_hi(q, tile):
                act.wait_ge(merged, q * KT + tile + 1)
                act.wait_ge(half_job, done(q, YB, 0))
                copy(m_hi[:, tile, :], gb[:, tile, :]).then_inc(m_hi_ready, 1)

            def input_squares(n):
                act.wait_ge(xs_loaded, 16 * (n - TT + 1))
                act.wait_ge(h_ready, n)
                nc.scalar.activation(t_flat, xs, ACT.Square, scale=D ** -0.5, accum_out=mean[:, 0:1]).then_inc(x_mean, 1)

            def input_hi(n, t, src):
                act.wait_ge(h_transposed, n + 1)
                copy(h_hi[:, :, bass.ds(t * P, P)], src).then_inc(h_hi_ready, 1)

            def squares_y(n, src, dst, column):
                act.wait_ge(y_transposed, n + 1)
                nc.scalar.activation(dst, src, ACT.Square, scale=D ** -0.5,
                                     accum_out=mean[:, column:column + 1]).then_inc(y_mean, 1)

            def store_rows(n, row):
                act.dma_start(out[bass.ds(n * P, P), :], row).then_inc(out_stored, 16)

            def attention_gate(q, pair, k):
                act.wait_ge(half_job, done(q, pair, k))
                nc.scalar.activation(silu_tmp[k], gemm[k][:, :], ACT.Sigmoid).then_inc(gate_sig, 1)

            def store_y(n, row):
                act.wait_ge(y_summed, n + 1)
                store_rows(n, row)

            def head(q, before):
                rotate(q, KV, 0)
                act.wait_ge(half_job, done(q, KV, 1))
                copy(v_raw, gemm[1][:, :]).then_inc(bank_free[1], 1)
                act.wait_ge(kv_carried, q + 1)
                act.wait_ge(roped, q * ROPED + 1)
                for g in range(KVH):
                    for half in range(2):
                        ins = copy(kk[HD * half:HD * (half + 1), g, 0, P:P + T], qr[0][HD * g:HD * (g + 1), :])
                ins.then_inc(rope_hi, 1)
                rotate(q, Q, 0)
                if before is not None:
                    squares_y(before * TT, t_flat, y_squares, TT)
                rotate(q, Q, 1)
                q_hi(q, 1, 0, 0)
                with act.Fori(1, TT) as i:
                    rotate(q, Q + i, 0)
                    if before is not None:
                        store_y(before * TT + i - 1, x_last[:, i - 1, :])
                        squares_y(before * TT + i, t_flat, y_squares, TT)
                    q_hi(q, 2 * i, 1, 4 * i - 2)
                    rotate(q, Q + i, 1)
                    q_hi(q, 2 * i + 1, 0, 4 * i)
                act.wait_ge(v_transposed, q + 1)
                copy(vv[:, 1:1 + TT, :, 0:HD], v_ps[:, :, :, :]).then_inc(v_hi_ready, 1)
                attention_gate(q, ZA, 0)
                q_hi(q, 2 * TT, 1, HEADS - 2)
                if before is not None:
                    store_y(before * TT + TT - 1, x_last[:, TT - 1, :])
                attention_gate(q, ZA, 1)

            def conv_c(q, c):
                act.wait_ge(half_job, done(q, CONV + 2 * c, 0))
                copy(c_in, gemm[0][:, :]).then_inc(bank_free[0], 1)

            def conv_gate(q, c):
                act.wait_ge(half_job, done(q, CONV + 2 * c + 1, 1))
                nc.scalar.activation(c_gate, gemm[1][:, :], ACT.Sigmoid).then_inc(z_sig, 1)
                act.wait_ge(ua_mixed, q * KT + c + 1)
                copy(m_hi[:, c, :], c_y).then_inc(ua_hi_ready, 1)

            def quarter(q, last):
                with act.Fori(ZA + 1, GATES - 1) as pair:
                    for k in range(2):
                        attention_gate(q, pair, k)
                attention_gate(q, GATES - 1, 0)
                exps(q, 0, 0)
                attention_gate(q, GATES - 1, 1)

                def copy_gate(row, pair, k):
                    act.wait_ge(half_job, done(q, pair, k))
                    copy(gates[:, row, :], gemm[k][:, :]).then_inc(bank_free[k], 1)

                copy_gate(0, GATES, 0)
                split_p(q, 0, 0)
                exps(q, 1, 1)
                copy_gate(1, GATES, 1)

                def attention_step(i):
                    for g, pair, more_scores, more_transposes in steps(i):
                        u, k = GROUPS * i + g, g % 2
                        move_o(q, u)
                        if more_transposes:
                            split_p(q, u + 1, 1 - k)
                        if more_scores:
                            exps(q, u + LEAD, k)
                        ub_hi(q, u, i, g)
                        if more_scores:
                            copy_gate(u + LEAD, pair, k)
                        elif k == 0:
                            conv_c(q, 0)

                with act.Fori(0, TT - 1) as i:
                    attention_step(i)
                attention_step(TT - 1)
                conv_gate(q, 0)
                with act.Fori(1, KT) as c:
                    act.wait_ge(bank_free[1], freed(q, CONV + 2 * c - 1))
                    conv_c(q, c)
                    conv_gate(q, c)
                for first, row, evac in ((YA, 0, False), (YB, KT, True)):
                    if last:
                        with act.Fori(0, KT) as tile:
                            merge_sigmoid(row + tile)
                            if evac:
                                yb_hi(q, tile)
                    else:
                        with act.Fori(0, TT // 2) as i:
                            n = TT * (q + 1) + (first - YA) // 2 + i
                            for k in range(4):
                                merge_sigmoid(row + 4 * i + k)
                                if evac:
                                    yb_hi(q, 4 * i + k)
                                if k == 0:
                                    input_squares(n)
                                if k == 2:
                                    input_hi(n, (first - YA) // 2 + i, t_ps[:, :, :])
                with act.Fori(0, KT // 2) as i:
                    for k in range(2):
                        act.wait_ge(half_job, done(q, Y + i, k))
                        copy(za[:, 2 * i + k, :], gemm[k][:, :]).then_inc(bank_free[k], 1)
                if not last:
                    head(q + 1, q)
                else:
                    for t in range(TT):
                        squares_y(q * TT + t, row_flat[t], y_out[:, t, :], TT + t)
                    for t in (1, 0, 2, 3):
                        if t == 0:
                            act.wait_ge(y_added, 1)
                        else:
                            act.wait_ge(y_summed, q * TT + t)
                        store_rows(q * TT + t, y_out[:, t, :])
                act.wait_ge(out_stored, (q + 1) * TT * 16)

            def first_squares(t):
                act.wait_ge(x_first_loaded[t], 16)
                nc.scalar.activation(y_out[:, t, :], x_first[:, t, :], ACT.Square, scale=D ** -0.5,
                                     accum_out=mean[:, t:t + 1]).then_inc(x_mean, 1)

            first_squares(0)
            first_squares(1)
            input_hi(0, 0, row_tiles[0])
            for t in range(2, TT):
                first_squares(t)
            for t in range(1, TT):
                input_hi(t, t, row_tiles[t])
            head(0, None)
            with act.Fori(0, NQ - 1) as q:
                quarter(q, False)
            quarter(NQ - 1, True)

        @block.vector
        def _(dve):
            def mult(dst, a, b):
                return nc.vector.tensor_tensor(dst, a, b, ALU.mult)

            def minus(dst, a, b):
                return nc.vector.tensor_tensor(dst, a, b, ALU.subtract)

            def split_weights(loads, k):
                dve.wait_ge(w_loaded[k], 16 * loads)
                for half in range(2):
                    lo, hi = half * KT // 2, (half + 1) * KT // 2
                    nc.vector.tensor_copy(w_hi[k][:, lo:hi, :],
                                          w_raw[:, k, lo * P:hi * P].rearrange("p (c n) -> p c n", n=P))\
                        .then_inc(w_hi_ready, 1)

            def next_weights(q, pair, k):
                dve.wait_ge(half_job, done(q, pair, k))
                split_weights(freed(q, pair) + 1, k)

            def add_rope(q, pair, k, n):
                dve.wait_ge(rot_ready, q * ROPED + n + 1)
                mult(qr[k], gemm[k][:, :], rope[:, 0, :]).then_inc(bank_free[k], 1)

            def finish_rope(q, pair, k, n):
                dve.wait_ge(rot_scaled, q * ROPED + n + 1)
                dve.wait_ge(bank_free[k], freed(q, pair))
                nc.vector.tensor_add(qr[k], qr[k], rot[k]).then_inc(roped, 1)

            def q_lo(q, n, k, head):
                dve.wait_ge(rope_hi, q * ROPED + n + 1)
                minus(qu[HD:P, head, :], qr[k][0:HD, :], f32(qu[0:HD, head, :]))
                minus(qu[0:HD, head + 1, :], qr[k][HD:P, :], f32(qu[HD:P, head + 1, :])).then_inc(rope_lo, 1)

            def scale_scores(q, u, k, g):
                if not isinstance(u, int) or u >= 2:
                    dve.wait_ge(pt_ready, unit(q, u) - 2)
                dve.wait_ge(scores_ready, unit(q, u))
                nc.vector.memset(carrier[:, :], 0.0)
                for head in range(UNIT_HEADS):
                    n = UNIT_HEADS * g + head
                    ins = nc.vector.tensor_tensor_reduce(
                        out=prob[k][:, head, :], in0=s_ps[:, head, :], in1=mask[:, :, :].rearrange("p a k -> p (a k)"),
                        scale=HD ** -0.5, scalar=sink[:, n:n + 1], op0=ALU.add, op1=ALU.max,
                        accum_out=rowmax[:, k, head:head + 1])
                ins.then_inc(scores_used, 1)
                dve.wait_ge(scores_used, unit(q, u))
                minus(sinkd[:, k, :], sink[:, UNIT_HEADS * g:UNIT_HEADS * (g + 1)], rowmax[:, k, :])
                nc.vector.tensor_scalar(negmax[:, k, :], rowmax[:, k, :], -1.0, None, ALU.mult)\
                    .then_inc(negmax_ready, 1)

            def denominators(q, u, k):
                dve.wait_ge(exp_done, unit(q, u))
                nc.vector.tensor_add(denom[:, k, :], rowsum[:, k, :], sinkd[:, k, :]).then_inc(denom_ready, 1)
                dve.wait_ge(denom_ready, unit(q, u))
                nc.vector.reciprocal(rden[:, k, :], denom[:, k, :]).then_inc(rden_ready, 1)

            def split_p(q, u, k):
                dve.wait_ge(pt_hi_ready, unit(q, u))
                minus(pt_lo[k], t_flat.rearrange("p (a n) -> p a n", a=2), f32(pt_hi[k])).then_inc(pt_lo_ready, 1)

            def gate_o(q, u, b, g):
                dve.wait_ge(o_moved, unit(q, u))
                if g > 0:
                    dve.wait_ge(ub_ready, unit(q, u) - 1)
                nc.vector.tensor_add(att[0:HD, :, :], o_ps[0:HD, 0:UNIT_HEADS:2, :], otmp[0:HD, :, :])
                nc.vector.tensor_add(att[HD:P, :, :], o_ps[HD:P, 1:UNIT_HEADS:2, :], otmp[HD:P, :, :])\
                    .then_inc(o_added, 1)
                dve.wait_ge(o_added, unit(q, u))
                mult(att[:, :, :], att[:, :, :], za[:, 2 * g:2 * g + 2, bass.ds(b * P, P)]).then_inc(ub_gated, 1)

            def ub_lo(q, u, b, g):
                dve.wait_ge(ub_hi_ready, unit(q, u))
                row, cols = UNIT_HEADS * g, bass.ds(b * P, P)
                minus(qu[:, row + 1:row + UNIT_HEADS:2, cols], att[:, :, :], f32(qu[:, row:row + UNIT_HEADS:2, cols]))\
                    .then_inc(ub_ready, 1)

            def norm_input(n, src, column):
                dve.wait_ge(x_rstd, n + 1)
                nc.vector.scalar_tensor_tensor(src, src, rstd[:, column:column + 1], gpre[:, :], ALU.mult, ALU.mult)\
                    .then_inc(x_normed, 1)

            def input_lo(n, t, src):
                dve.wait_ge(h_hi_ready, n + 1)
                minus(h_lo[:, :, bass.ds(t * P, P)], src, f32(h_hi[:, :, bass.ds(t * P, P)])).then_inc(h_ready, 1)

            def merge_a(q, pair, k, tile):
                next_weights(q, pair, k)
                dve.wait_ge(merge_sig, 2 * KT * q + tile + 1)
                mult(ga[:, tile, :], gemm[k][:, :], ga[:, tile, :]).then_inc(bank_free[k], 1)

            def merge_b(q, pair, k, tile):
                next_weights(q, pair, k)
                dve.wait_ge(merge_sig, 2 * KT * q + KT + tile + 1)
                mult(gb[:, tile, :], gemm[k][:, :], gb[:, tile, :]).then_inc(bank_free[k], 1)
                dve.wait_ge(bank_free[k], freed(q, pair))
                nc.vector.tensor_add(gb[:, tile, :], gb[:, tile, :], ga[:, tile, :]).then_inc(merged, 1)
                dve.wait_ge(m_hi_ready, q * KT + tile + 1)
                minus(m_lo[:, tile, :], gb[:, tile, :], f32(m_hi[:, tile, :])).then_inc(m_ready, 1)

            def scale_y(n, src, column, scaled):
                dve.wait_ge(y_rstd, n + 1)
                nc.vector.scalar_tensor_tensor(scaled, src, rstd[:, column:column + 1], gpost, ALU.mult, ALU.mult)\
                    .then_inc(y_scaled, 1)

            def finish_y(n, t, src, column, scaled, total):
                scale_y(n, src, column, scaled)
                dve.wait_ge(y_scaled, n + 1)
                nc.vector.tensor_add(total, scaled, x_last[:, t, :]).then_inc(y_summed, 1)

            def attention_gate(q, i, k):
                dve.wait_ge(gate_sig, q * KT + 2 * i + k + 1)
                mult(za[:, 2 * i + k, :], gemm[k][:, :], silu_tmp[k]).then_inc(bank_free[k], 1)

            def head(q, before):
                nc.vector.tensor_copy(kk[:, :, :, 0:P], f32(kk[:, :, :, T:T + P]))
                nc.vector.tensor_copy(vv[:, 0, :, :], f32(vv[:, TT, :, :])).then_inc(kv_carried, 1)
                next_weights(q, KV, 0)
                dve.wait_ge(rope_loaded, 16 * (q + 1))
                add_rope(q, KV, 0, 0)
                next_weights(q, KV, 1)
                finish_rope(q, KV, 0, 0)
                next_weights(q, Q, 0)
                dve.wait_ge(rope_hi, q * ROPED + 1)
                for g in range(KVH):
                    own = slice(HD * g, HD * (g + 1))
                    for half in range(2):
                        ins = minus(kk[HD * half:HD * (half + 1), g, 1, P:P + T], qr[0][own, :],
                                    f32(kk[own, g, 0, P:P + T]))
                ins.then_inc(rope_lo, 1)

                dve.wait_ge(rope_lo, q * ROPED + 1)
                add_rope(q, Q, 0, 1)
                next_weights(q, Q, 1)
                finish_rope(q, Q, 0, 1)
                add_rope(q, Q, 1, 2)
                if before is not None:
                    dve.wait_ge(tail_loaded, 32 * (before + 1))
                    finish_y(before * TT, 0, t_flat, TT, y_scaled_row, x_last[:, 0, :])
                with dve.Fori(1, TT) as i:
                    next_weights(q, Q + i, 0)
                    q_lo(q, 2 * i - 1, 0, 4 * i - 4)
                    finish_rope(q, Q + i - 1, 1, 2 * i)
                    dve.wait_ge(rope_lo, q * ROPED + 2 * i)
                    add_rope(q, Q + i, 0, 2 * i + 1)
                    next_weights(q, Q + i, 1)
                    q_lo(q, 2 * i, 1, 4 * i - 2)
                    finish_rope(q, Q + i, 0, 2 * i + 1)
                    dve.wait_ge(rope_lo, q * ROPED + 2 * i + 1)
                    add_rope(q, Q + i, 1, 2 * i + 2)
                    if before is not None:
                        finish_y(before * TT + i, i, t_flat, TT, y_scaled_row, x_last[:, i, :])
                next_weights(q, ZA, 0)
                q_lo(q, 2 * TT - 1, 0, HEADS - 4)
                finish_rope(q, ZA - 1, 1, 2 * TT)
                attention_gate(q, 0, 0)
                next_weights(q, ZA, 1)
                q_lo(q, 2 * TT, 1, HEADS - 2)
                attention_gate(q, 0, 1)
                dve.wait_ge(v_hi_ready, q + 1)
                minus(vv[:, 1:1 + TT, :, HD:2 * HD], v_ps[:, :, :, :], f32(vv[:, 1:1 + TT, :, 0:HD]))\
                    .then_inc(v_ready, 1)

            def conv_taps(q, c):
                pair, tap = CONV + 2 * c, 3 * (q * KT + c)
                nc.vector.tensor_copy(c_u[:, 0:2], halo[:, c, :]).then_inc(halo_in, 1)
                dve.wait_ge(bank_free[0], freed(q, pair))
                mult(c_u[:, 2:T + 2], gemm[1][:, :], c_in).then_inc(bank_free[1], 1)
                dve.wait_ge(halo_in, q * KT + c + 1)
                dve.wait_ge(bank_free[1], freed(q, pair))
                nc.vector.tensor_scalar(c_y, c_u[:, 0:T], taps[:, c, 0:1], None, ALU.mult).then_inc(tap_done, 1)
                nc.vector.tensor_copy(halo[:, c, :], c_u[:, T:T + 2])
                dve.wait_ge(tap_done, tap + 1)
                nc.vector.scalar_tensor_tensor(c_y, c_u[:, 1:T + 1], taps[:, c, 1:2], c_y, ALU.mult, ALU.add)\
                    .then_inc(tap_done, 1)
                dve.wait_ge(tap_done, tap + 2)
                nc.vector.scalar_tensor_tensor(c_y, c_u[:, 2:T + 2], taps[:, c, 2:3], c_y, ALU.mult, ALU.add)\
                    .then_inc(tap_done, 1)

            def conv_gate(q, c):
                pair = CONV + 2 * c + 1
                next_weights(q, pair, 0)
                dve.wait_ge(tap_done, 3 * (q * KT + c) + 3)
                mult(c_y, gemm[0][:, :], c_y).then_inc(bank_free[0], 1)
                next_weights(q, pair, 1)
                dve.wait_ge(z_sig, q * KT + c + 1)
                mult(c_gate, gemm[1][:, :], c_gate).then_inc(bank_free[1], 1)
                dve.wait_ge(bank_free[1], freed(q, pair))
                mult(c_y, c_y, c_gate).then_inc(ua_mixed, 1)
                dve.wait_ge(ua_hi_ready, q * KT + c + 1)
                minus(m_lo[:, c, :], c_y, f32(m_hi[:, c, :])).then_inc(ua_ready, 1)

            def quarter(q, last):
                with dve.Fori(1, KT // 2 - 1) as i:
                    for k in range(2):
                        next_weights(q, ZA + i, k)
                        attention_gate(q, i, k)
                next_weights(q, GATES - 1, 0)
                attention_gate(q, KT // 2 - 1, 0)
                scale_scores(q, 0, 0, 0)
                denominators(q, 0, 0)
                next_weights(q, GATES - 1, 1)
                attention_gate(q, KT // 2 - 1, 1)
                next_weights(q, GATES, 0)
                scale_scores(q, 1, 1, 1)
                split_p(q, 0, 0)
                denominators(q, 1, 1)
                next_weights(q, GATES, 1)

                def attention_step(i):
                    for g, pair, more_scores, more_transposes in steps(i):
                        u, k = GROUPS * i + g, g % 2
                        if more_scores:
                            scale_scores(q, u + LEAD, k, (g + LEAD) % GROUPS)
                            if g + LEAD == GROUPS - 1:
                                nc.vector.tensor_copy(mask[:, 0, :], band[:, 0, :]).then_inc(mask_full, 1)
                        gate_o(q, u, i, g)
                        if more_transposes:
                            split_p(q, u + 1, 1 - k)
                        if more_scores:
                            denominators(q, u + LEAD, k)
                        ub_lo(q, u, i, g)
                        next_weights(q, pair, k)

                with dve.Fori(0, TT - 1) as i:
                    attention_step(i)
                attention_step(TT - 1)

                conv_taps(q, 0)
                conv_gate(q, 0)
                with dve.Fori(1, KT) as c:
                    for k in range(2):
                        next_weights(q, CONV + 2 * c, k)
                    conv_taps(q, c)
                    conv_gate(q, c)
                for first, merge in ((YA, merge_a), (YB, merge_b)):
                    if last:
                        with dve.Fori(0, KT // 2) as i:
                            for k in range(2):
                                merge(q, first + i, k, 2 * i + k)
                    else:
                        with dve.Fori(0, TT // 2) as i:
                            n = TT * (q + 1) + (first - YA) // 2 + i
                            for k in range(4):
                                if k == 2:
                                    norm_input(n, xs, 0)
                                if k == 3:
                                    input_lo(n, (first - YA) // 2 + i, t_ps[:, :, :])
                                merge(q, first + 2 * i + k // 2, k % 2, 4 * i + k)
                if last:
                    with dve.Fori(Y, PAIRS - 1) as pair:
                        for k in range(2):
                            next_weights(q, pair, k)
                else:
                    with dve.Fori(Y, PAIRS) as pair:
                        for k in range(2):
                            next_weights(q, pair, k)
                if not last:
                    head(q + 1, q)
                    return
                dve.wait_ge(tail_loaded, 32 * (q + 1))
                scale_y(q * TT, row_flat[0], TT, y_out[:, 0, :])
                for t in range(1, TT):
                    finish_y(q * TT + t, t, row_flat[t], TT + t, y_out[:, t, :], y_out[:, t, :])

            nc.vector.memset(halo[:, :, :], 0.0)
            nc.vector.memset(kk[:, :, :, T:T + P].bitcast(F32), 0.0)
            nc.vector.memset(vv[:, TT, :, :].bitcast(F32), 0.0).then_inc(kv_zeroed, 1)
            dve.wait_ge(gain_loaded, 2 * 16)
            def first_norm(t):
                norm_input(t, x_first[:, t, :], t)

            first_norm(0)
            first_norm(1)
            input_lo(0, 0, row_tiles[0])
            for t in range(2, TT):
                first_norm(t)
            split_weights(1, 0)
            for t in range(1, TT):
                input_lo(t, t, row_tiles[t])
            split_weights(1, 1)
            dve.wait_ge(kv_zeroed, 1)
            dve.wait_ge(consts_loaded, N_CONSTS)
            head(0, None)
            with dve.Fori(0, NQ - 1) as q:
                quarter(q, False)
            quarter(NQ - 1, True)

        @block.gpsimd
        def _(pool):
            def split_weights(before, k):
                for half in range(2):
                    lo, hi = half * KT // 2, (half + 1) * KT // 2
                    pool.wait_ge(w_hi_ready, before + half + 1)
                    nc.gpsimd.tensor_tensor(w_lo[k][:, lo:hi, :],
                                            w_raw[:, k, lo * P:hi * P].rearrange("p (c n) -> p c n", n=P),
                                            f32(w_hi[k][:, lo:hi, :]), ALU.subtract).then_inc(w_lo_ready, 1)

            def next_weights(q, pair, k):
                split_weights(done(q, pair, k) + 2, k)

            def next_pairs(q, first, end):
                with pool.Fori(first, end) as pair:
                    for k in range(2):
                        next_weights(q, pair, k)

            def scale_rot(q, n, k):
                pool.wait_ge(rot_ready, q * ROPED + n + 1)
                nc.gpsimd.tensor_tensor(rot[k], rot[k], rope[:, 1, :], ALU.mult).then_inc(rot_scaled, 1)

            def normalise(q, u, k):
                pool.wait_ge(rden_ready, unit(q, u))
                nc.gpsimd.tensor_tensor(prob[k], prob[k],
                                        rden[:, k, :].unsqueeze(2).broadcast_to([P, UNIT_HEADS, 2 * P]),
                                        ALU.mult).then_inc(probs_ready, 1)

            def inverse_root(column, n, mean_sem, msq_sem, rstd_sem):
                cols = slice(column, column + 1)
                pool.wait_ge(mean_sem, n + 1)
                nc.gpsimd.tensor_tensor(msq[:, cols], mean[:, cols], root_consts[:, 1:2], ALU.add).then_inc(msq_sem, 1)
                pool.wait_ge(msq_sem, n + 1)
                nc.gpsimd.tensor_tensor(rstd[:, cols], msq[:, cols], root_consts[:, 0:1], ALU.pow).then_inc(rstd_sem, 1)

            def head(q, before):
                next_weights(q, KV, 0)
                pool.wait_ge(rope_loaded, 16 * (q + 1))
                scale_rot(q, 0, 0)
                next_weights(q, KV, 1)
                with pool.Fori(0, TT) as i:
                    next_weights(q, Q + i, 0)
                    scale_rot(q, 1 + 2 * i, 0)
                    if before is not None:
                        inverse_root(TT, before * TT + i, y_mean, y_msq, y_rstd)
                    next_weights(q, Q + i, 1)
                    scale_rot(q, 2 + 2 * i, 1)
                for k in range(2):
                    next_weights(q, ZA, k)

            def quarter(q, last):
                next_pairs(q, ZA + 1, GATES - 1)
                for k in range(2):
                    next_weights(q, GATES - 1, k)
                    if k == 0:
                        normalise(q, 0, 0)
                for k in range(2):
                    next_weights(q, GATES, k)
                    if k == 0:
                        normalise(q, 1, 1)

                def attention_step(i):
                    for g, pair, more_scores, _ in steps(i):
                        if more_scores:
                            normalise(q, GROUPS * i + g + LEAD, g % 2)
                        next_weights(q, pair, g % 2)

                with pool.Fori(0, TT - 1) as i:
                    attention_step(i)
                attention_step(TT - 1)
                next_pairs(q, CONV + 1, YA)
                if last:
                    next_pairs(q, YA, PAIRS - 1)
                else:
                    with pool.Fori(0, TT) as t:
                        next_weights(q, YA + 2 * t, 0)
                        inverse_root(0, TT * (q + 1) + t, x_mean, x_msq, x_rstd)
                        next_weights(q, YA + 2 * t, 1)
                        next_weights(q, YA + 2 * t + 1, 0)
                        next_weights(q, YA + 2 * t + 1, 1)
                    next_pairs(q, Y, PAIRS)
                    head(q + 1, q)
                    return
                for t in range(TT):
                    inverse_root(TT + t, q * TT + t, y_mean, y_msq, y_rstd)
                pool.wait_ge(y_scaled, q * TT + 1)
                nc.gpsimd.tensor_tensor(y_out[:, 0, :], y_out[:, 0, :], x_last[:, 0, :], ALU.add).then_inc(y_added, 1)

            nc.gpsimd.memset(root_consts[:, 0:1], -0.5)
            nc.gpsimd.memset(root_consts[:, 1:2], EPS).then_inc(root_consts_set, 1)
            pool.wait_ge(root_consts_set, 1)
            for t in range(TT):
                inverse_root(t, t, x_mean, x_msq, x_rstd)
            for k in range(2):
                split_weights(2 * k, k)
            head(0, None)
            with pool.Fori(0, NQ - 1) as q:
                quarter(q, False)
            quarter(NQ - 1, True)


def weight_tiles(w_in, w_proj_conv, w_proj_attn, w_out):
    widths = (D, D, D, D, D, KVH * HD, KVH * HD, D, D, D)
    ends = np.cumsum(widths)
    xc, bg, cg, zc, q, k, v, za, ga, gb = (w_in[:, e - w:e] for e, w in zip(ends, widths))
    cols = [k, v, q, za, ga, gb]
    for c in range(KT):
        cols += [m[:, c * P:(c + 1) * P] for m in (cg, xc, bg, zc)]
    cols += [w_proj_conv, w_proj_attn, w_out]
    w = np.concatenate(cols, axis=1)
    return np.ascontiguousarray(w.reshape(KT, P, JOBS, P).transpose(2, 1, 0, 3).reshape(JOBS, P, D))


def rope_tables():
    inv = (10000.0 ** (-np.arange(0, HD, 2, dtype=np.float32) / np.float32(HD))).astype(np.float32)
    angle = (np.arange(SEQ, dtype=np.float32)[:, None] * inv[None, :]).astype(np.float32).astype(np.float64)
    cos, sin = np.cos(angle).T, np.sin(angle).T
    both = np.stack([np.concatenate([cos] * 4), np.concatenate([-sin, sin] * 2)], axis=1)
    return np.ascontiguousarray(both.reshape(P, 2, NQ, T).transpose(2, 0, 1, 3).reshape(NQ, P, 2 * T).astype(np.float32))


def mask_table():
    qi, kj = np.arange(P)[:, None], np.arange(P)[None, :]
    previous = np.where(kj > qi, 0.0, MASKED)
    own = np.where(kj <= qi, 0.0, MASKED)
    return np.concatenate([np.eye(P), previous, own, np.full((P, P), MASKED), own], axis=1).astype(np.float32)


def kernel(x, g_pre, g_post, w_in, w_conv, sinks, w_proj_conv, w_proj_attn, w_out):
    import concourse.bacc as bacc
    from concourse.bass_utils import run_bass_kernel_spmd

    arrays = {
        "x": np.ascontiguousarray(np.asarray(x)[0]),
        "wjobs": weight_tiles(*(np.asarray(w)[0] for w in (w_in, w_proj_conv, w_proj_attn, w_out))),
        "g_pre": np.ascontiguousarray(np.asarray(g_pre)),
        "g_post": np.ascontiguousarray(np.asarray(g_post)),
        "w_conv": np.ascontiguousarray(np.asarray(w_conv)[0].reshape(3, KT, P).transpose(2, 1, 0)),
        "sinks": np.ascontiguousarray(np.asarray(sinks)),
        "tables": rope_tables(),
        "masks": mask_table(),
    }
    nc = bacc.Bacc("TRN2", target_bir_lowering=False, num_devices=1)
    args = [nc.dram_tensor(name, a.shape, F32, kind="ExternalInput").ap() for name, a in arrays.items()]
    out = nc.dram_tensor("out", (SEQ, D), F32, kind="ExternalOutput").ap()
    build(nc, *args, out)
    result = run_bass_kernel_spmd(nc, [arrays], core_ids=[0])
    return result.results[0]["out"].reshape(1, SEQ, D)
```

```python
from contextlib import ExitStack

import numpy as np

import concourse.bass as bass
from concourse import mybir

F32 = mybir.dt.float32
F32R = mybir.dt.float32r
ACT = mybir.ActivationFunctionType
ALU = mybir.AluOpType

P = 128
SEQ, D = 2048, 1024
KT = D // P
T = 512
NQ = SEQ // T
TT = T // P
HEADS, HD, KVH = 16, 64, 2
UNIT_HEADS = 4
GROUPS = HEADS // UNIT_HEADS
UNITS = TT * GROUPS
EPS = 1e-6
MASKED = -1e30

KV, Q, ZA, GATES, CONV, YA, YB, Y, PAIRS = 0, 1, 5, 9, 17, 33, 37, 41, 45
JOBS = 2 * PAIRS
SLABS = 4
LEAD = 2
ROPED = 1 + HEADS // 2


def build(nc, x, wjobs, g_pre, g_post, w_conv, sinks, tables, masks, out):
    ctx = ExitStack()
    with ctx:
        def sbuf(name, shape, dtype=F32):
            return ctx.enter_context(nc.sbuf_tensor(name, shape, dtype))

        def psum(name, shape):
            return ctx.enter_context(nc.psum_tensor(name, shape, F32))

        def sem(name):
            return ctx.enter_context(nc.semaphore(name))

        h_hi = sbuf("h_hi", [P, KT, T], F32R)
        h_lo = sbuf("h_lo", [P, KT, T], F32R)
        qu = sbuf("qu", [P, HEADS, T], F32R)
        m_hi = sbuf("m_hi", [P, KT, T], F32R)
        m_lo = sbuf("m_lo", [P, KT, T], F32R)
        za = sbuf("za", [P, KT, T])
        gates = sbuf("gates", [P, 2 * KT, T])
        ga, gb = gates[:, 0:KT, :], gates[:, KT:2 * KT, :]
        w_raw = sbuf("w_raw", [P, 2, D])
        w_hi = [sbuf(f"w_hi{i}", [P, KT, P], F32R) for i in range(2)]
        w_lo = [sbuf(f"w_lo{i}", [P, KT, P], F32R) for i in range(2)]
        kk = sbuf("kk", [P, KVH, 2, P + T], F32R)
        vv = sbuf("vv", [P, 1 + TT, KVH, 2 * HD], F32R)
        rope = sbuf("rope", [P, 2, T])
        band = sbuf("band", [P, 2, P])
        mask = sbuf("mask", [P, 2, P])
        ident = sbuf("ident", [P, P])
        side = sbuf("side", [P, 2, P])
        gpre = sbuf("gpre", [P, D])
        taps = sbuf("taps", [P, KT, 3])
        sink = sbuf("sink", [P, HEADS])
        halo = sbuf("halo", [P, KT, 2])
        otmp = sbuf("otmp", [P, 2, P])
        att = sbuf("att", [P, 2, P])
        rowmax = sbuf("rowmax", [P, 2, UNIT_HEADS])
        negmax = sbuf("negmax", [P, 2, UNIT_HEADS])
        sinkd = sbuf("sinkd", [P, 2, UNIT_HEADS])
        rowsum = sbuf("rowsum", [P, 2, UNIT_HEADS])
        denom = sbuf("denom", [P, 2, UNIT_HEADS])
        rden = sbuf("rden", [P, 2, UNIT_HEADS])
        mean = sbuf("mean", [P, 3 * TT])
        msq = sbuf("msq", [P, 2 * TT])
        rstd = sbuf("rstd", [P, 2 * TT])
        root_consts = sbuf("root_consts", [P, 2])
        carrier = sbuf("carrier", [P, 1])
        work = sbuf("work", [P, 4 * T + 2])

        def f32(ap):
            return ap.bitcast(F32)

        prob = [work[:, i * 2 * T:(i + 1) * 2 * T].rearrange("p (h k) -> p h k", h=UNIT_HEADS)
                for i in range(2)]
        merged_p = [p[:, :, 0:P] for p in prob]
        merged_hi = [p[:, :, P:2 * P] for p in prob]
        c_in, c_y, c_gate = (work[:, i * T:(i + 1) * T] for i in range(3))
        c_u = work[:, 3 * T:4 * T + 2]
        xs = gpost = work[:, 0:D]
        v_raw = gb[:, 0, :]
        rot = [gb[:, 1 + i, :] for i in range(2)]
        qr = [gb[:, (3, 6)[i], :] for i in range(2)]
        silu_tmp = [gb[:, 4 + i, :] for i in range(2)]

        def token_rows(tensor):
            return tensor.rearrange("p (t a) n -> p t (a n)", t=TT)

        x_first, x_last, y_gained = token_rows(za[:, :, :]), token_rows(ga), token_rows(za[:, :, :])
        squares = gb
        pt_hi = [m_hi[:, 2 * i:2 * i + 2, :] for i in range(2)]
        pt_lo = [m_lo[:, 2 * i:2 * i + 2, :] for i in range(2)]

        gemm_ps = psum("gemm_ps", [P, 2, T])
        gemm = [gemm_ps[:, k, :] for k in range(2)]
        left_ps = psum("left_ps", [P, TT, T])
        s_flat, t_flat = (left_ps[:, 2 * i:2 * i + 2, :].rearrange("p k t -> p (k t)") for i in range(2))
        s_ps = s_flat.rearrange("p (h k) -> p h k", h=UNIT_HEADS)
        t_ps = t_flat.rearrange("p (c n) -> p c n", n=P)
        pt_ps = [t_ps[:, UNIT_HEADS * i:UNIT_HEADS * (i + 1), :] for i in range(2)]
        ov_ps = psum("ov_ps", [P, 2, T])
        o_flat = ov_ps[:, 0, :]
        o_ps = o_flat.rearrange("p (h t) -> p h t", h=UNIT_HEADS)
        v_ps = ov_ps[:, 1, :].rearrange("p (b g d) -> p b g d", b=TT, g=KVH)
        right_ps = [gemm[0], gemm[1], ov_ps[:, 0, :], ov_ps[:, 1, :]]
        row_tiles = [flat.rearrange("p (c n) -> p c n", n=P) for flat in
                     [s_flat, t_flat] + [ps[:, :, :].rearrange("p k t -> p (k t)") for ps in (ov_ps, gemm_ps)]]

        gain_loaded = sem("gain_loaded")
        consts_loaded = sem("consts_loaded")
        kv_zeroed = sem("kv_zeroed")
        root_consts_set = sem("root_consts_set")
        w_loaded = [sem(f"w_loaded{i}") for i in range(2)]
        w_hi_ready = sem("w_hi_ready")
        w_lo_ready = sem("w_lo_ready")
        half_job = sem("half_job")
        bank_free = [sem(f"bank_free{i}") for i in range(2)]
        x_first_loaded = [sem(f"x_first_loaded{t}") for t in range(TT)]
        xs_loaded = sem("xs_loaded")
        x_mean = sem("x_mean")
        x_msq = sem("x_msq")
        x_rstd = sem("x_rstd")
        x_normed = sem("x_normed")
        h_transposed = sem("h_transposed")
        h_hi_ready = sem("h_hi_ready")
        h_ready = sem("h_ready")
        rope_loaded = sem("rope_loaded")
        kv_carried = sem("kv_carried")
        rot_ready = sem("rot_ready")
        rot_scaled = sem("rot_scaled")
        roped = sem("roped")
        rope_hi = sem("rope_hi")
        rope_lo = sem("rope_lo")
        v_transposed = sem("v_transposed")
        v_hi_ready = sem("v_hi_ready")
        v_ready = sem("v_ready")
        gate_sig = sem("gate_sig")
        scores_ready = sem("scores_ready")
        scores_used = sem("scores_used")
        mask_full = sem("mask_full")
        negmax_ready = sem("negmax_ready")
        exp_done = sem("exp_done")
        denom_ready = sem("denom_ready")
        rden_ready = sem("rden_ready")
        probs_ready = sem("probs_ready")
        pt_ready = sem("pt_ready")
        merged_hi_ready = sem("merged_hi_ready")
        merged_lo_ready = sem("merged_lo_ready")
        pt_hi_ready = sem("pt_hi_ready")
        pt_lo_ready = sem("pt_lo_ready")
        o_ready = sem("o_ready")
        o_moved = sem("o_moved")
        o_added = sem("o_added")
        ub_gated = sem("ub_gated")
        ub_hi_ready = sem("ub_hi_ready")
        ub_ready = sem("ub_ready")
        halo_in = sem("halo_in")
        tap_done = sem("tap_done")
        z_sig = sem("z_sig")
        ua_mixed = sem("ua_mixed")
        ua_hi_ready = sem("ua_hi_ready")
        ua_ready = sem("ua_ready")
        merge_sig = sem("merge_sig")
        merged = sem("merged")
        m_hi_ready = sem("m_hi_ready")
        m_ready = sem("m_ready")
        tail_loaded = sem("tail_loaded")
        y_mean = sem("y_mean")
        y_left_gained = sem("y_left_gained")
        y_right_gained = sem("y_right_gained")
        y_msq = sem("y_msq")
        y_rstd = sem("y_rstd")
        y_summed = sem("y_summed")
        out_stored = sem("out_stored")
        N_CONSTS = 5 * 16

        def both_blocks(square):
            return square.unsqueeze(1).broadcast_to([P, 2, UNIT_HEADS, P])

        side_of_heads = side[:, :, :].unsqueeze(2).broadcast_to([P, 2, UNIT_HEADS, P])

        def by_head(pt):
            return pt.rearrange("p a (h n) -> p a h n", h=UNIT_HEADS)

        def done(q, pair, k):
            return q * 2 * JOBS + pair * 4 + 2 * k + 2

        def freed(q, pair):
            return q * (Y + 1) + pair + 1

        def loaded(q, pair):
            return q * PAIRS + pair + 1

        def unit(q, u):
            return q * UNITS + u + 1

        def steps(i):
            last = isinstance(i, int)
            for g in range(GROUPS):
                yield (g, GATES + 2 * i + (g + LEAD) // 2, not (last and g + LEAD >= GROUPS),
                       not (last and g + 1 >= GROUPS))

        block = ctx.enter_context(nc.Block())

        @block.sync
        def _(sp):
            for t in range(TT):
                sp.dma_start(x_first[:, t, :], x[t * P:(t + 1) * P, :]).then_inc(x_first_loaded[t], 16)
                if t == 0:
                    sp.dma_start(gpre[:, :], g_pre.broadcast_to([P, D])).then_inc(gain_loaded, 16)
                    sp.dma_start(ident[:, :], masks[:, 0:P]).then_inc(gain_loaded, 16)
            for k in range(2):
                sp.dma_start(w_raw[:, k, :], wjobs[k]).then_inc(w_loaded[k], 16)
            sp.dma_start(band[:, :, :], masks[:, P:3 * P].rearrange("p (a k) -> p a k", a=2)).then_inc(consts_loaded, 16)
            sp.dma_start(mask[:, :, :], masks[:, 3 * P:5 * P].rearrange("p (a k) -> p a k", a=2)).then_inc(consts_loaded, 16)
            sp.dma_start(side[:, :, :], masks[:, 5 * P:7 * P].rearrange("p (a k) -> p a k", a=2)).then_inc(consts_loaded, 16)
            sp.dma_start(taps[:, :, :], w_conv).then_inc(consts_loaded, 16)
            sp.dma_start(sink[:, :], sinks.broadcast_to([P, HEADS])).then_inc(consts_loaded, 16)

            def load_pair(q, pair, nxt):
                for k in range(2):
                    sp.wait_ge(w_lo_ready, done(q, pair, k))
                    sp.dma_start(w_raw[:, k, :], wjobs[2 * nxt + k]).then_inc(w_loaded[k], 16)

            def loads(q, first, end):
                with sp.Fori(first, end) as pair:
                    load_pair(q, pair, pair + 1)

            def load_rope(q):
                sp.dma_start(rope[:, :, :], tables[q].rearrange("p (a t) -> p a t", a=2)).then_inc(rope_loaded, 16)

            def quarter(q, last):
                loads(q, 0, YA)
                if not last:
                    sp.wait_ge(roped, (q + 1) * ROPED)
                    load_rope(q + 1)
                if last:
                    loads(q, YA, Y + 1)
                else:
                    with sp.Fori(0, TT) as t:
                        load_pair(q, YA + 2 * t, YA + 2 * t + 1)
                        sp.wait_ge(ua_ready, KT * (q + 1))
                        sp.wait_ge(h_transposed, TT * (q + 1) + t)
                        sp.dma_start(xs, x[bass.ds((q + 1) * T + t * P, P), :]).then_inc(xs_loaded, 16)
                        load_pair(q, YA + 2 * t + 1, YA + 2 * t + 2)
                    load_pair(q, Y, Y + 1)
                sp.wait_ge(m_ready, KT * (q + 1))
                if not last:
                    sp.wait_ge(h_transposed, TT * (q + 2))
                sp.dma_start(gpost, g_post.broadcast_to([P, D])).then_inc(tail_loaded, 16)
                sp.dma_start(x_last, x[bass.ds(q * T, T), :].rearrange("(t p) d -> p t d", p=P)).then_inc(tail_loaded, 16)
                loads(q, Y + 1, PAIRS - 1)
                if not last:
                    load_pair(q, PAIRS - 1, 0)

            load_rope(0)
            with sp.Fori(0, NQ - 1) as q:
                quarter(q, False)
            quarter(NQ - 1, True)

        @block.tensor
        def _(pe):
            def job(q, pair, k, hi, lo, tiles=None, per_quarter=KT, first=False):
                if tiles is not None:
                    pe.wait_ge(tiles, per_quarter * (q + 1) - 1)
                if not first:
                    pe.wait_ge(bank_free[k], freed(q, pair) - 1)
                for kt in range(KT):
                    if kt % (KT // 2) == 0:
                        pe.wait_ge(w_lo_ready, done(q, pair, k) - 1 + kt // (KT // 2))
                    if kt == KT - 1 and tiles is not None:
                        pe.wait_ge(tiles, per_quarter * (q + 1))
                    for n, (w, moving) in enumerate(((w_lo[k], hi), (w_hi[k], lo), (w_hi[k], hi))):
                        ins = nc.tensor.matmul(gemm[k][:, :], w[:, kt, :], moving[:, kt, :],
                                               start=kt == 0 and n == 0, stop=kt == KT - 1 and n == 2)
                    if kt % (KT // 2) == KT // 2 - 1:
                        ins.then_inc(half_job, 1)

            def jobs(q, first, end, *operand):
                with pe.Fori(first, end) as pair:
                    for k in range(2):
                        job(q, pair, k, *operand)

            h, m = (h_hi, h_lo), (m_hi, m_lo)
            ub = (qu[:, 0:HEADS:2, :], qu[:, 1:HEADS:2, :])

            def transpose_h(ready, src, dst, read=0):
                pe.wait_ge(x_normed, ready)
                if read:
                    pe.wait_ge(h_ready, read)
                for c in range(KT):
                    ins = nc.tensor.transpose(dst[:, c, :], src[:, c * P:(c + 1) * P], ident[:, :])
                ins.then_inc(h_transposed, 1)

            def scores(q, u):
                b, g = divmod(u, GROUPS)
                if u == 0:
                    pe.wait_ge(rope_lo, (q + 1) * ROPED)
                if u > 0:
                    pe.wait_ge(scores_used, unit(q, u) - 1)
                for head in range(UNIT_HEADS):
                    for part in (1, 0):
                        ins = nc.tensor.matmul(s_ps[:, head, :], qu[:, UNIT_HEADS * g + head, b * P:(b + 1) * P],
                                               kk[:, g // 2, part, b * P:(b + 2) * P], start=part == 1, stop=part == 0)
                ins.then_inc(scores_ready, 1)

            def transpose_p(q, u):
                pe.wait_ge(probs_ready, unit(q, u))
                for head in range(UNIT_HEADS):
                    ins = nc.tensor.transpose(pt_ps[u % 2][:, head, :], merged_p[u % 2][:, head, :], ident[:, :])
                ins.then_inc(pt_ready, 1)

            def values(q, u):
                b, g = divmod(u, GROUPS)
                pe.wait_ge(pt_hi_ready, unit(q, u))
                pe.wait_ge(pt_lo_ready, unit(q, u))
                if u > 0:
                    pe.wait_ge(o_added, unit(q, u) - 1)
                if u == 0:
                    pe.wait_ge(v_ready, q + 1)
                for n in range(4):
                    part, pt = n // 2, (pt_lo, pt_hi)[n % 2][u % 2]
                    ins = nc.tensor.matmul(o_flat, vv[:, b + part, g // 2, :],
                                           pt[:, part, :], start=n == 0, stop=n == 3)
                ins.then_inc(o_ready, 1)

            def output_job(q, j, last):
                half, slab = divmod(j, SLABS)
                pair, k = Y + j // 2, j % 2
                w = [w_part[k][:, :, :].rearrange("p (a c) n -> p a (c n)", a=2) for w_part in (w_hi, w_lo)]
                pe.wait_ge(w_lo_ready, done(q, pair, k) - 1)
                if half == 0:
                    pe.wait_ge(m_ready, q * KT + 2 * slab + 2)
                if j == SLABS:
                    for parity in range(2):
                        pe.wait_ge(bank_free[parity], freed(q, Y - 1))
                for t in range(TT):
                    bank = right_ps[t] if half else left_ps[:, t, :]
                    if j == 0 and t == 2 and not last:
                        pe.wait_ge(h_ready, TT * (q + 2))
                    for a in range(2):
                        if t == 0 and a == 1:
                            pe.wait_ge(w_lo_ready, done(q, pair, k))
                        for n, (m_part, w_part) in enumerate(((m_lo, w[0]), (m_hi, w[1]), (m_hi, w[0]))):
                            ins = nc.tensor.matmul(bank, m_part[:, 2 * slab + a, t * P:(t + 1) * P], w_part[:, a, :],
                                                   start=slab == 0 and a == 0 and n == 0,
                                                   stop=slab == SLABS - 1 and a == 1 and n == 2)
                    if t % 2 == 1:
                        ins.then_inc(half_job, 1)

            def head(q, before):
                pe.wait_ge(h_ready, TT * (q + 1))
                for k in range(2):
                    job(q, KV, k, *h, first=before is None)
                jobs(q, Q, ZA, *h)
                if before is not None:
                    pe.wait_ge(y_right_gained, 2 * (before + 1))
                pe.wait_ge(bank_free[1], freed(q, KV))
                for b in range(TT):
                    ins = nc.tensor.transpose(v_ps[:, b, :, :].rearrange("p g d -> p (g d)"),
                                              v_raw[:, b * P:(b + 1) * P], ident[:, :])
                ins.then_inc(v_transposed, 1)
                for k in range(2):
                    job(q, ZA, k, *h)

            def quarter(q, last):
                jobs(q, ZA + 1, GATES - 1, *h)
                job(q, GATES - 1, 0, *h)
                scores(q, 0)
                job(q, GATES - 1, 1, *h)
                for s in range(-LEAD, UNITS):
                    if 0 < s + LEAD < UNITS:
                        scores(q, s + LEAD)
                    if s >= 0:
                        values(q, s)
                    if 0 <= s + 1 < UNITS:
                        transpose_p(q, s + 1)
                    job(q, GATES + (s + LEAD) // 2, s % 2, *h)
                jobs(q, CONV + 1, YA, *h)
                for first, operand in ((YA, (*m, ua_ready)), (YB, (*ub, ub_ready, UNITS))):
                    if last:
                        jobs(q, first, first + KT // 2, *operand)
                    else:
                        with pe.Fori(0, TT // 2) as i:
                            job(q, first + 2 * i, 0, *operand)
                            job(q, first + 2 * i, 1, *operand)
                            job(q, first + 2 * i + 1, 0, *operand)
                            transpose_h(TT * (q + 1) + (first - YA) // 2 + i + 1, xs, t_ps)
                            job(q, first + 2 * i + 1, 1, *operand)
                for j in range(2 * SLABS):
                    output_job(q, j, last)
                if not last:
                    head(q + 1, q)

            pe.wait_ge(gain_loaded, 2 * 16)
            for t in range(TT):
                transpose_h(t + 1, x_first[:, t, :], row_tiles[t])
            head(0, None)
            with pe.Fori(0, NQ - 1) as q:
                quarter(q, False)
            quarter(NQ - 1, True)

        @block.scalar
        def _(act):
            def copy(dst, src):
                return nc.scalar.activation(dst, src, ACT.Copy)

            def rotate(q, pair, k):
                act.wait_ge(half_job, done(q, pair, k))
                for a in range(4):
                    b = a ^ 1
                    ins = copy(rot[k][32 * b:32 * b + 32, :], gemm[k][32 * a:32 * a + 32, :])
                ins.then_inc(rot_ready, 1)

            def q_hi(q, n, k, head):
                act.wait_ge(roped, q * ROPED + n + 1)
                copy(qu[0:HD, head, :], qr[k][0:HD, :])
                copy(qu[HD:P, head + 1, :], qr[k][HD:P, :]).then_inc(rope_hi, 1)

            def exps(q, u, k):
                act.wait_ge(negmax_ready, unit(q, u))
                for head in range(UNIT_HEADS):
                    nc.scalar.activation(merged_p[k][:, head, :], merged_p[k][:, head, :], ACT.Exp,
                                         bias=negmax[:, k, head:head + 1], accum_out=rowsum[:, k, head:head + 1])
                nc.scalar.activation(sinkd[:, k, :], sinkd[:, k, :], ACT.Exp).then_inc(exp_done, 1)

            def split_p(q, u, k):
                act.wait_ge(pt_ready, unit(q, u))
                copy(merged_hi[k].bitcast(F32R), pt_ps[k]).then_inc(merged_hi_ready, 1)

            def move_o(q, u):
                act.wait_ge(o_ready, unit(q, u))
                copy(otmp[0:HD, :, :], o_ps[HD:P, 0:UNIT_HEADS:2, :])
                copy(otmp[HD:P, :, :], o_ps[0:HD, 1:UNIT_HEADS:2, :]).then_inc(o_moved, 1)

            def ub_hi(q, u, b, g):
                act.wait_ge(ub_gated, unit(q, u))
                copy(qu[:, UNIT_HEADS * g:UNIT_HEADS * (g + 1):2, bass.ds(b * P, P)], att[:, :, :])\
                    .then_inc(ub_hi_ready, 1)

            def merge_sigmoid(row):
                nc.scalar.activation(gates[:, row, :], gates[:, row, :], ACT.Sigmoid).then_inc(merge_sig, 1)

            def yb_hi(q, tile):
                act.wait_ge(merged, q * KT + tile + 1)
                act.wait_ge(half_job, done(q, YB, 0))
                copy(m_hi[:, tile, :], gb[:, tile, :]).then_inc(m_hi_ready, 1)

            def input_squares(n):
                act.wait_ge(xs_loaded, 16 * (n - TT + 1))
                act.wait_ge(h_ready, n)
                nc.scalar.activation(t_flat, xs, ACT.Square, scale=D ** -0.5, accum_out=mean[:, 0:1]).then_inc(x_mean, 1)

            def input_hi(n, t, src):
                act.wait_ge(h_transposed, n + 1)
                copy(h_hi[:, :, bass.ds(t * P, P)], src).then_inc(h_hi_ready, 1)

            def squares_y(src, column):
                nc.scalar.activation(squares[:, column - TT, :], src, ACT.Square, scale=D ** -0.5,
                                     accum_out=mean[:, column:column + 1]).then_inc(y_mean, 1)

            def store_rows(n, row):
                act.dma_start(out[bass.ds(n * P, P), :], row).then_inc(out_stored, 16)

            def attention_gate(q, pair, k):
                act.wait_ge(half_job, done(q, pair, k))
                nc.scalar.activation(silu_tmp[k], gemm[k][:, :], ACT.Sigmoid).then_inc(gate_sig, 1)

            def store_y(n, row):
                act.wait_ge(y_summed, n + 1)
                store_rows(n, row)

            def head(q, before):
                rotate(q, KV, 0)
                act.wait_ge(half_job, done(q, KV, 1))
                copy(v_raw, gemm[1][:, :]).then_inc(bank_free[1], 1)
                act.wait_ge(kv_carried, q + 1)
                act.wait_ge(roped, q * ROPED + 1)
                for g in range(KVH):
                    for half in range(2):
                        ins = copy(kk[HD * half:HD * (half + 1), g, 0, P:P + T], qr[0][HD * g:HD * (g + 1), :])
                ins.then_inc(rope_hi, 1)
                rotate(q, Q, 0)
                rotate(q, Q, 1)
                q_hi(q, 1, 0, 0)
                with act.Fori(1, TT) as i:
                    rotate(q, Q + i, 0)
                    if before is not None:
                        store_y(before * TT + i - 1, x_last[:, i - 1, :])
                    q_hi(q, 2 * i, 1, 4 * i - 2)
                    rotate(q, Q + i, 1)
                    q_hi(q, 2 * i + 1, 0, 4 * i)
                act.wait_ge(v_transposed, q + 1)
                copy(vv[:, 1:1 + TT, :, 0:HD], v_ps[:, :, :, :]).then_inc(v_hi_ready, 1)
                attention_gate(q, ZA, 0)
                q_hi(q, 2 * TT, 1, HEADS - 2)
                if before is not None:
                    store_y(before * TT + TT - 1, x_last[:, TT - 1, :])
                attention_gate(q, ZA, 1)

            def conv_c(q, c):
                act.wait_ge(half_job, done(q, CONV + 2 * c, 0))
                copy(c_in, gemm[0][:, :]).then_inc(bank_free[0], 1)

            def conv_gate(q, c):
                act.wait_ge(half_job, done(q, CONV + 2 * c + 1, 1))
                nc.scalar.activation(c_gate, gemm[1][:, :], ACT.Sigmoid).then_inc(z_sig, 1)
                act.wait_ge(ua_mixed, q * KT + c + 1)
                copy(m_hi[:, c, :], c_y).then_inc(ua_hi_ready, 1)

            def quarter(q, last):
                with act.Fori(ZA + 1, GATES - 1) as pair:
                    for k in range(2):
                        attention_gate(q, pair, k)
                attention_gate(q, GATES - 1, 0)
                exps(q, 0, 0)
                attention_gate(q, GATES - 1, 1)

                def copy_gate(row, pair, k):
                    act.wait_ge(half_job, done(q, pair, k))
                    copy(gates[:, row, :], gemm[k][:, :]).then_inc(bank_free[k], 1)

                copy_gate(0, GATES, 0)
                split_p(q, 0, 0)
                exps(q, 1, 1)
                copy_gate(1, GATES, 1)

                def attention_step(i):
                    for g, pair, more_scores, more_transposes in steps(i):
                        u, k = GROUPS * i + g, g % 2
                        move_o(q, u)
                        if more_transposes:
                            split_p(q, u + 1, 1 - k)
                        if more_scores:
                            exps(q, u + LEAD, k)
                        ub_hi(q, u, i, g)
                        if more_scores:
                            copy_gate(u + LEAD, pair, k)
                        elif k == 0:
                            conv_c(q, 0)

                with act.Fori(0, TT - 1) as i:
                    attention_step(i)
                attention_step(TT - 1)
                conv_gate(q, 0)
                with act.Fori(1, KT) as c:
                    act.wait_ge(bank_free[1], freed(q, CONV + 2 * c - 1))
                    conv_c(q, c)
                    conv_gate(q, c)
                for first, row, evac in ((YA, 0, False), (YB, KT, True)):
                    if last:
                        with act.Fori(0, KT) as tile:
                            merge_sigmoid(row + tile)
                            if evac:
                                yb_hi(q, tile)
                    else:
                        with act.Fori(0, TT // 2) as i:
                            n = TT * (q + 1) + (first - YA) // 2 + i
                            for k in range(4):
                                merge_sigmoid(row + 4 * i + k)
                                if evac:
                                    yb_hi(q, 4 * i + k)
                                if k == 0:
                                    input_squares(n)
                                if k == 2:
                                    input_hi(n, (first - YA) // 2 + i, t_ps[:, :, :])
                act.wait_ge(half_job, done(q, Y + 1, 1))
                for t in range(TT):
                    squares_y(left_ps[:, t, :], TT + t)
                for t in range(TT):
                    if t % 2 == 0:
                        act.wait_ge(half_job, done(q, PAIRS - 1, 1) - 1 + t // 2)
                    squares_y(right_ps[t], 2 * TT + t)
                if not last:
                    head(q + 1, q)
                else:
                    for t in range(TT):
                        store_y(q * TT + t, x_last[:, t, :])
                act.wait_ge(out_stored, (q + 1) * TT * 16)

            def first_squares(t):
                act.wait_ge(x_first_loaded[t], 16)
                nc.scalar.activation(token_rows(squares)[:, t, :], x_first[:, t, :], ACT.Square, scale=D ** -0.5,
                                     accum_out=mean[:, t:t + 1]).then_inc(x_mean, 1)

            first_squares(0)
            first_squares(1)
            input_hi(0, 0, row_tiles[0])
            for t in range(2, TT):
                first_squares(t)
            for t in range(1, TT):
                input_hi(t, t, row_tiles[t])
            head(0, None)
            with act.Fori(0, NQ - 1) as q:
                quarter(q, False)
            quarter(NQ - 1, True)

        @block.vector
        def _(dve):
            def mult(dst, a, b):
                return nc.vector.tensor_tensor(dst, a, b, ALU.mult)

            def minus(dst, a, b):
                return nc.vector.tensor_tensor(dst, a, b, ALU.subtract)

            def split_weights(loads, k):
                dve.wait_ge(w_loaded[k], 16 * loads)
                for half in range(2):
                    lo, hi = half * KT // 2, (half + 1) * KT // 2
                    nc.vector.tensor_copy(w_hi[k][:, lo:hi, :],
                                          w_raw[:, k, lo * P:hi * P].rearrange("p (c n) -> p c n", n=P))\
                        .then_inc(w_hi_ready, 1)

            def next_weights(q, pair, k):
                dve.wait_ge(half_job, done(q, pair, k))
                split_weights(loaded(q, pair) + 1, k)

            def add_rope(q, pair, k, n):
                dve.wait_ge(rot_ready, q * ROPED + n + 1)
                mult(qr[k], gemm[k][:, :], rope[:, 0, :]).then_inc(bank_free[k], 1)

            def finish_rope(q, pair, k, n):
                dve.wait_ge(rot_scaled, q * ROPED + n + 1)
                dve.wait_ge(bank_free[k], freed(q, pair))
                nc.vector.tensor_add(qr[k], qr[k], rot[k]).then_inc(roped, 1)

            def q_lo(q, n, k, head):
                dve.wait_ge(rope_hi, q * ROPED + n + 1)
                minus(qu[HD:P, head, :], qr[k][0:HD, :], f32(qu[0:HD, head, :]))
                minus(qu[0:HD, head + 1, :], qr[k][HD:P, :], f32(qu[HD:P, head + 1, :])).then_inc(rope_lo, 1)

            def scale_scores(q, u, k, g):
                if not isinstance(u, int) or u >= 2:
                    dve.wait_ge(pt_hi_ready, unit(q, u) - 2)
                    dve.wait_ge(pt_lo_ready, unit(q, u) - 2)
                dve.wait_ge(scores_ready, unit(q, u))
                nc.vector.memset(carrier[:, :], 0.0)
                for head in range(UNIT_HEADS):
                    n = UNIT_HEADS * g + head
                    ins = nc.vector.tensor_tensor_reduce(
                        out=prob[k][:, head, :], in0=s_ps[:, head, :], in1=mask[:, :, :].rearrange("p a k -> p (a k)"),
                        scale=HD ** -0.5, scalar=sink[:, n:n + 1], op0=ALU.add, op1=ALU.max,
                        accum_out=rowmax[:, k, head:head + 1])
                ins.then_inc(scores_used, 1)
                dve.wait_ge(scores_used, unit(q, u))
                minus(sinkd[:, k, :], sink[:, UNIT_HEADS * g:UNIT_HEADS * (g + 1)], rowmax[:, k, :])
                nc.vector.tensor_scalar(negmax[:, k, :], rowmax[:, k, :], -1.0, None, ALU.mult)
                nc.vector.tensor_tensor(merged_p[k], prob[k][:, :, 0:P], prob[k][:, :, P:2 * P], ALU.max)\
                    .then_inc(negmax_ready, 1)

            def denominators(q, u, k):
                dve.wait_ge(exp_done, unit(q, u))
                nc.vector.tensor_add(denom[:, k, :], rowsum[:, k, :], sinkd[:, k, :]).then_inc(denom_ready, 1)
                dve.wait_ge(denom_ready, unit(q, u))
                nc.vector.reciprocal(rden[:, k, :], denom[:, k, :]).then_inc(rden_ready, 1)

            def split_p(q, u, k):
                dve.wait_ge(merged_hi_ready, unit(q, u))
                minus(merged_p[k], pt_ps[k], merged_hi[k]).then_inc(merged_lo_ready, 1)

            def part_lo(q, u, k):
                dve.wait_ge(merged_lo_ready, unit(q, u))
                mult(by_head(pt_lo[k]), both_blocks(merged_p[k]), side_of_heads).then_inc(pt_lo_ready, 1)

            def gate_o(q, u, b, g):
                dve.wait_ge(o_moved, unit(q, u))
                if g > 0:
                    dve.wait_ge(ub_ready, unit(q, u) - 1)
                nc.vector.tensor_add(att[0:HD, :, :], o_ps[0:HD, 0:UNIT_HEADS:2, :], otmp[0:HD, :, :])
                nc.vector.tensor_add(att[HD:P, :, :], o_ps[HD:P, 1:UNIT_HEADS:2, :], otmp[HD:P, :, :])\
                    .then_inc(o_added, 1)
                dve.wait_ge(o_added, unit(q, u))
                mult(att[:, :, :], att[:, :, :], za[:, 2 * g:2 * g + 2, bass.ds(b * P, P)]).then_inc(ub_gated, 1)

            def ub_lo(q, u, b, g):
                dve.wait_ge(ub_hi_ready, unit(q, u))
                row, cols = UNIT_HEADS * g, bass.ds(b * P, P)
                minus(qu[:, row + 1:row + UNIT_HEADS:2, cols], att[:, :, :], f32(qu[:, row:row + UNIT_HEADS:2, cols]))\
                    .then_inc(ub_ready, 1)

            def norm_input(n, src, column):
                dve.wait_ge(x_rstd, n + 1)
                nc.vector.scalar_tensor_tensor(src, src, rstd[:, column:column + 1], gpre[:, :], ALU.mult, ALU.mult)\
                    .then_inc(x_normed, 1)

            def input_lo(n, t, src):
                dve.wait_ge(h_hi_ready, n + 1)
                minus(h_lo[:, :, bass.ds(t * P, P)], src, f32(h_hi[:, :, bass.ds(t * P, P)])).then_inc(h_ready, 1)

            def merge_a(q, pair, k, tile):
                next_weights(q, pair, k)
                dve.wait_ge(merge_sig, 2 * KT * q + tile + 1)
                mult(ga[:, tile, :], gemm[k][:, :], ga[:, tile, :]).then_inc(bank_free[k], 1)

            def merge_b(q, pair, k, tile):
                next_weights(q, pair, k)
                dve.wait_ge(merge_sig, 2 * KT * q + KT + tile + 1)
                mult(gb[:, tile, :], gemm[k][:, :], gb[:, tile, :]).then_inc(bank_free[k], 1)
                dve.wait_ge(bank_free[k], freed(q, pair))
                nc.vector.tensor_add(gb[:, tile, :], gb[:, tile, :], ga[:, tile, :]).then_inc(merged, 1)
                dve.wait_ge(m_hi_ready, q * KT + tile + 1)
                minus(m_lo[:, tile, :], gb[:, tile, :], f32(m_hi[:, tile, :])).then_inc(m_ready, 1)

            def gain_left(q, t):
                dve.wait_ge(y_mean, 2 * q * TT + t + 1)
                mult(y_gained[:, t, 0:T], left_ps[:, t, :], gpost[:, 0:T]).then_inc(y_left_gained, 1)

            def gain_right(q, t):
                dve.wait_ge(y_mean, (2 * q + 1) * TT + t + 1)
                mult(y_gained[:, t, T:D], right_ps[t], gpost[:, T:D])\
                    .then_inc(bank_free[t] if t < 2 else y_right_gained, 1)

            def finish_y(q, t):
                nc.vector.scalar_tensor_tensor(x_last[:, t, :], y_gained[:, t, :], rstd[:, bass.ds(TT + t, 1)],
                                               x_last[:, t, :], ALU.mult, ALU.add).then_inc(y_summed, 1)

            def attention_gate(q, i, k):
                dve.wait_ge(gate_sig, q * KT + 2 * i + k + 1)
                mult(za[:, 2 * i + k, :], gemm[k][:, :], silu_tmp[k]).then_inc(bank_free[k], 1)

            def head(q, before):
                nc.vector.tensor_copy(kk[:, :, :, 0:P], f32(kk[:, :, :, T:T + P]))
                nc.vector.tensor_copy(vv[:, 0, :, :], f32(vv[:, TT, :, :])).then_inc(kv_carried, 1)
                next_weights(q, KV, 0)
                dve.wait_ge(rope_loaded, 16 * (q + 1))
                add_rope(q, KV, 0, 0)
                next_weights(q, KV, 1)
                finish_rope(q, KV, 0, 0)
                next_weights(q, Q, 0)
                dve.wait_ge(rope_hi, q * ROPED + 1)
                for g in range(KVH):
                    own = slice(HD * g, HD * (g + 1))
                    for half in range(2):
                        ins = minus(kk[HD * half:HD * (half + 1), g, 1, P:P + T], qr[0][own, :],
                                    f32(kk[own, g, 0, P:P + T]))
                ins.then_inc(rope_lo, 1)

                dve.wait_ge(rope_lo, q * ROPED + 1)
                add_rope(q, Q, 0, 1)
                next_weights(q, Q, 1)
                finish_rope(q, Q, 0, 1)
                add_rope(q, Q, 1, 2)
                if before is not None:
                    dve.wait_ge(y_rstd, before + 1)
                    dve.wait_ge(y_right_gained, 2 * (before + 1))
                    finish_y(before, 0)
                with dve.Fori(1, TT) as i:
                    next_weights(q, Q + i, 0)
                    q_lo(q, 2 * i - 1, 0, 4 * i - 4)
                    finish_rope(q, Q + i - 1, 1, 2 * i)
                    dve.wait_ge(rope_lo, q * ROPED + 2 * i)
                    add_rope(q, Q + i, 0, 2 * i + 1)
                    next_weights(q, Q + i, 1)
                    q_lo(q, 2 * i, 1, 4 * i - 2)
                    finish_rope(q, Q + i, 0, 2 * i + 1)
                    dve.wait_ge(rope_lo, q * ROPED + 2 * i + 1)
                    add_rope(q, Q + i, 1, 2 * i + 2)
                    if before is not None:
                        finish_y(before, i)
                next_weights(q, ZA, 0)
                q_lo(q, 2 * TT - 1, 0, HEADS - 4)
                finish_rope(q, ZA - 1, 1, 2 * TT)
                attention_gate(q, 0, 0)
                next_weights(q, ZA, 1)
                q_lo(q, 2 * TT, 1, HEADS - 2)
                attention_gate(q, 0, 1)
                dve.wait_ge(v_hi_ready, q + 1)
                minus(vv[:, 1:1 + TT, :, HD:2 * HD], v_ps[:, :, :, :], f32(vv[:, 1:1 + TT, :, 0:HD]))\
                    .then_inc(v_ready, 1)

            def conv_taps(q, c):
                pair, tap = CONV + 2 * c, 3 * (q * KT + c)
                nc.vector.tensor_copy(c_u[:, 0:2], halo[:, c, :]).then_inc(halo_in, 1)
                dve.wait_ge(bank_free[0], freed(q, pair))
                mult(c_u[:, 2:T + 2], gemm[1][:, :], c_in).then_inc(bank_free[1], 1)
                dve.wait_ge(halo_in, q * KT + c + 1)
                dve.wait_ge(bank_free[1], freed(q, pair))
                nc.vector.tensor_scalar(c_y, c_u[:, 0:T], taps[:, c, 0:1], None, ALU.mult).then_inc(tap_done, 1)
                nc.vector.tensor_copy(halo[:, c, :], c_u[:, T:T + 2])
                dve.wait_ge(tap_done, tap + 1)
                nc.vector.scalar_tensor_tensor(c_y, c_u[:, 1:T + 1], taps[:, c, 1:2], c_y, ALU.mult, ALU.add)\
                    .then_inc(tap_done, 1)
                dve.wait_ge(tap_done, tap + 2)
                nc.vector.scalar_tensor_tensor(c_y, c_u[:, 2:T + 2], taps[:, c, 2:3], c_y, ALU.mult, ALU.add)\
                    .then_inc(tap_done, 1)

            def conv_gate(q, c):
                pair = CONV + 2 * c + 1
                next_weights(q, pair, 0)
                dve.wait_ge(tap_done, 3 * (q * KT + c) + 3)
                mult(c_y, gemm[0][:, :], c_y).then_inc(bank_free[0], 1)
                next_weights(q, pair, 1)
                dve.wait_ge(z_sig, q * KT + c + 1)
                mult(c_gate, gemm[1][:, :], c_gate).then_inc(bank_free[1], 1)
                dve.wait_ge(bank_free[1], freed(q, pair))
                mult(c_y, c_y, c_gate).then_inc(ua_mixed, 1)
                dve.wait_ge(ua_hi_ready, q * KT + c + 1)
                minus(m_lo[:, c, :], c_y, f32(m_hi[:, c, :])).then_inc(ua_ready, 1)

            def quarter(q, last):
                with dve.Fori(1, KT // 2 - 1) as i:
                    for k in range(2):
                        next_weights(q, ZA + i, k)
                        attention_gate(q, i, k)
                next_weights(q, GATES - 1, 0)
                attention_gate(q, KT // 2 - 1, 0)
                scale_scores(q, 0, 0, 0)
                denominators(q, 0, 0)
                next_weights(q, GATES - 1, 1)
                attention_gate(q, KT // 2 - 1, 1)
                next_weights(q, GATES, 0)
                scale_scores(q, 1, 1, 1)
                split_p(q, 0, 0)
                denominators(q, 1, 1)
                part_lo(q, 0, 0)
                next_weights(q, GATES, 1)

                def attention_step(i):
                    for g, pair, more_scores, more_transposes in steps(i):
                        u, k = GROUPS * i + g, g % 2
                        if more_scores:
                            scale_scores(q, u + LEAD, k, (g + LEAD) % GROUPS)
                            if g + LEAD == GROUPS - 1:
                                nc.vector.tensor_copy(mask[:, 0, :], band[:, 0, :]).then_inc(mask_full, 1)
                        gate_o(q, u, i, g)
                        if more_transposes:
                            split_p(q, u + 1, 1 - k)
                        if more_scores:
                            denominators(q, u + LEAD, k)
                        if more_transposes:
                            part_lo(q, u + 1, 1 - k)
                        ub_lo(q, u, i, g)
                        next_weights(q, pair, k)

                with dve.Fori(0, TT - 1) as i:
                    attention_step(i)
                attention_step(TT - 1)

                conv_taps(q, 0)
                conv_gate(q, 0)
                with dve.Fori(1, KT) as c:
                    for k in range(2):
                        next_weights(q, CONV + 2 * c, k)
                    conv_taps(q, c)
                    conv_gate(q, c)
                for first, merge in ((YA, merge_a), (YB, merge_b)):
                    if last:
                        with dve.Fori(0, KT // 2) as i:
                            for k in range(2):
                                merge(q, first + i, k, 2 * i + k)
                    else:
                        with dve.Fori(0, TT // 2) as i:
                            n = TT * (q + 1) + (first - YA) // 2 + i
                            for k in range(4):
                                if k == 2:
                                    norm_input(n, xs, 0)
                                if k == 3:
                                    input_lo(n, (first - YA) // 2 + i, t_ps[:, :, :])
                                merge(q, first + 2 * i + k // 2, k % 2, 4 * i + k)
                with dve.Fori(Y, Y + SLABS // 2) as pair:
                    for k in range(2):
                        next_weights(q, pair, k)
                dve.wait_ge(tail_loaded, 32 * (q + 1))
                for t in range(TT):
                    gain_left(q, t)
                    if t < 3 and not (last and t >= 2):
                        next_weights(q, Y + (SLABS + t) // 2, t % 2)
                gain_right(q, 0)
                gain_right(q, 1)
                if not last:
                    next_weights(q, PAIRS - 1, 1)
                    for t in range(2, TT):
                        gain_right(q, t)
                    head(q + 1, q)
                    return
                for t in range(TT):
                    if t == 0:
                        dve.wait_ge(bank_free[1], freed(q, Y))
                        dve.wait_ge(y_rstd, q + 1)
                    if t == 2:
                        for late in range(2, TT):
                            gain_right(q, late)
                        dve.wait_ge(y_right_gained, 2 * (q + 1))
                        dve.wait_ge(y_rstd, q + 2)
                    finish_y(q, t)

            nc.vector.memset(halo[:, :, :], 0.0)
            nc.vector.memset(kk[:, :, :, T:T + P].bitcast(F32), 0.0)
            nc.vector.memset(vv[:, TT, :, :].bitcast(F32), 0.0).then_inc(kv_zeroed, 1)
            dve.wait_ge(gain_loaded, 2 * 16)

            def first_norm(t):
                norm_input(t, x_first[:, t, :], t)

            first_norm(0)
            first_norm(1)
            input_lo(0, 0, row_tiles[0])
            for t in range(2, TT):
                first_norm(t)
            split_weights(1, 0)
            for t in range(1, TT):
                input_lo(t, t, row_tiles[t])
            split_weights(1, 1)
            dve.wait_ge(kv_zeroed, 1)
            dve.wait_ge(consts_loaded, N_CONSTS)
            head(0, None)
            with dve.Fori(0, NQ - 1) as q:
                quarter(q, False)
            quarter(NQ - 1, True)

        @block.gpsimd
        def _(pool):
            def split_weights(before, k):
                for half in range(2):
                    lo, hi = half * KT // 2, (half + 1) * KT // 2
                    pool.wait_ge(w_hi_ready, before + half + 1)
                    nc.gpsimd.tensor_tensor(w_lo[k][:, lo:hi, :],
                                            w_raw[:, k, lo * P:hi * P].rearrange("p (c n) -> p c n", n=P),
                                            f32(w_hi[k][:, lo:hi, :]), ALU.subtract).then_inc(w_lo_ready, 1)

            def next_weights(q, pair, k):
                split_weights(done(q, pair, k) + 2, k)

            def next_pairs(q, first, end):
                with pool.Fori(first, end) as pair:
                    for k in range(2):
                        next_weights(q, pair, k)

            def scale_rot(q, n, k):
                pool.wait_ge(rot_ready, q * ROPED + n + 1)
                nc.gpsimd.tensor_tensor(rot[k], rot[k], rope[:, 1, :], ALU.mult).then_inc(rot_scaled, 1)

            def normalise(q, u, k):
                pool.wait_ge(rden_ready, unit(q, u))
                nc.gpsimd.tensor_tensor(merged_p[k], merged_p[k],
                                        rden[:, k, :].unsqueeze(2).broadcast_to([P, UNIT_HEADS, P]),
                                        ALU.mult).then_inc(probs_ready, 1)

            def part_hi(q, u, k):
                pool.wait_ge(merged_hi_ready, unit(q, u))
                nc.gpsimd.tensor_tensor(by_head(pt_hi[k]), both_blocks(merged_hi[k]), side_of_heads, ALU.mult)\
                    .then_inc(pt_hi_ready, 1)

            def inverse_root(column, n, mean_sem, msq_sem, rstd_sem):
                cols = slice(column, column + 1)
                pool.wait_ge(mean_sem, n + 1)
                nc.gpsimd.tensor_tensor(msq[:, cols], mean[:, cols], root_consts[:, 1:2], ALU.add).then_inc(msq_sem, 1)
                pool.wait_ge(msq_sem, n + 1)
                nc.gpsimd.tensor_tensor(rstd[:, cols], msq[:, cols], root_consts[:, 0:1], ALU.pow).then_inc(rstd_sem, 1)

            def inverse_roots_y(means, n, t, end):
                left, right, cols = (slice(c + t, c + end) for c in (TT, 2 * TT, TT))
                pool.wait_ge(y_mean, means)
                nc.gpsimd.tensor_tensor(msq[:, cols], mean[:, left], mean[:, right], ALU.add).then_inc(y_msq, 1)
                pool.wait_ge(y_msq, 2 * n + 1)
                nc.gpsimd.tensor_tensor(msq[:, cols], msq[:, cols], root_consts[:, 1:2].broadcast_to([P, end - t]),
                                        ALU.add).then_inc(y_msq, 1)
                pool.wait_ge(y_msq, 2 * n + 2)
                nc.gpsimd.tensor_tensor(rstd[:, cols], msq[:, cols], root_consts[:, 0:1].broadcast_to([P, end - t]),
                                        ALU.pow).then_inc(y_rstd, 1)

            def head(q, before):
                next_weights(q, KV, 0)
                pool.wait_ge(rope_loaded, 16 * (q + 1))
                scale_rot(q, 0, 0)
                next_weights(q, KV, 1)
                if before is not None:
                    inverse_roots_y(2 * TT * (before + 1), before, 0, TT)
                with pool.Fori(0, TT) as i:
                    next_weights(q, Q + i, 0)
                    scale_rot(q, 1 + 2 * i, 0)
                    next_weights(q, Q + i, 1)
                    scale_rot(q, 2 + 2 * i, 1)
                for k in range(2):
                    next_weights(q, ZA, k)

            def quarter(q, last):
                next_pairs(q, ZA + 1, GATES - 1)
                for k in range(2):
                    next_weights(q, GATES - 1, k)
                    if k == 0:
                        normalise(q, 0, 0)
                for k in range(2):
                    next_weights(q, GATES, k)
                    if k == 0:
                        part_hi(q, 0, 0)
                        normalise(q, 1, 1)

                def attention_step(i):
                    for g, pair, more_scores, more_transposes in steps(i):
                        if more_transposes:
                            part_hi(q, GROUPS * i + g + 1, (g + 1) % 2)
                        if more_scores:
                            normalise(q, GROUPS * i + g + LEAD, g % 2)
                        next_weights(q, pair, g % 2)

                with pool.Fori(0, TT - 1) as i:
                    attention_step(i)
                attention_step(TT - 1)
                next_pairs(q, CONV + 1, YA)
                if last:
                    next_pairs(q, YA, PAIRS - 1)
                else:
                    with pool.Fori(0, TT) as t:
                        next_weights(q, YA + 2 * t, 0)
                        inverse_root(0, TT * (q + 1) + t, x_mean, x_msq, x_rstd)
                        next_weights(q, YA + 2 * t, 1)
                        next_weights(q, YA + 2 * t + 1, 0)
                        next_weights(q, YA + 2 * t + 1, 1)
                    next_pairs(q, Y, PAIRS)
                    head(q + 1, q)
                    return
                inverse_roots_y(2 * TT * q + TT + 2, q, 0, 2)
                inverse_roots_y(2 * TT * (q + 1), q + 1, 2, TT)

            nc.gpsimd.memset(root_consts[:, 0:1], -0.5)
            nc.gpsimd.memset(root_consts[:, 1:2], EPS).then_inc(root_consts_set, 1)
            pool.wait_ge(root_consts_set, 1)
            for t in range(TT):
                inverse_root(t, t, x_mean, x_msq, x_rstd)
            for k in range(2):
                split_weights(2 * k, k)
            head(0, None)
            with pool.Fori(0, NQ - 1) as q:
                quarter(q, False)
            quarter(NQ - 1, True)


def weight_tiles(w_in, w_proj_conv, w_proj_attn, w_out):
    widths = (D, D, D, D, D, KVH * HD, KVH * HD, D, D, D)
    ends = np.cumsum(widths)
    xc, bg, cg, zc, q, k, v, za, ga, gb = (w_in[:, e - w:e] for e, w in zip(ends, widths))
    cols = [k, v, q, za, ga, gb]
    for c in range(KT):
        cols += [m[:, c * P:(c + 1) * P] for m in (cg, xc, bg, zc)]
    cols += [w_proj_conv, w_proj_attn]
    w = np.concatenate(cols, axis=1)
    n = w.shape[1] // P
    tiles = w.reshape(KT, P, n, P).transpose(2, 1, 0, 3).reshape(n, P, D)
    out_tiles = w_out.reshape(SLABS, 2, P, 2, T).transpose(3, 0, 2, 1, 4).reshape(2 * SLABS, P, D)
    return np.ascontiguousarray(np.concatenate([tiles, out_tiles]))


def rope_tables():
    inv = (10000.0 ** (-np.arange(0, HD, 2, dtype=np.float32) / np.float32(HD))).astype(np.float32)
    angle = (np.arange(SEQ, dtype=np.float32)[:, None] * inv[None, :]).astype(np.float32).astype(np.float64)
    cos, sin = np.cos(angle).T, np.sin(angle).T
    both = np.stack([np.concatenate([cos] * 4), np.concatenate([-sin, sin] * 2)], axis=1)
    return np.ascontiguousarray(both.reshape(P, 2, NQ, T).transpose(2, 0, 1, 3).reshape(NQ, P, 2 * T).astype(np.float32))


def mask_table():
    qi, kj = np.arange(P)[:, None], np.arange(P)[None, :]
    previous = np.where(kj > qi, 0.0, MASKED)
    own = np.where(kj <= qi, 0.0, MASKED)
    return np.concatenate([np.eye(P), previous, own, np.full((P, P), MASKED), own,
                           (previous == 0.0).T, (own == 0.0).T], axis=1).astype(np.float32)


def kernel(x, g_pre, g_post, w_in, w_conv, sinks, w_proj_conv, w_proj_attn, w_out):
    import concourse.bacc as bacc
    from concourse.bass_utils import run_bass_kernel_spmd

    arrays = {
        "x": np.ascontiguousarray(np.asarray(x)[0]),
        "wjobs": weight_tiles(*(np.asarray(w)[0] for w in (w_in, w_proj_conv, w_proj_attn, w_out))),
        "g_pre": np.ascontiguousarray(np.asarray(g_pre)),
        "g_post": np.ascontiguousarray(np.asarray(g_post)),
        "w_conv": np.ascontiguousarray(np.asarray(w_conv)[0].reshape(3, KT, P).transpose(2, 1, 0)),
        "sinks": np.ascontiguousarray(np.asarray(sinks)),
        "tables": rope_tables(),
        "masks": mask_table(),
    }
    nc = bacc.Bacc("TRN2", target_bir_lowering=False, num_devices=1)
    args = [nc.dram_tensor(name, a.shape, F32, kind="ExternalInput").ap() for name, a in arrays.items()]
    out = nc.dram_tensor("out", (SEQ, D), F32, kind="ExternalOutput").ap()
    build(nc, *args, out)
    result = run_bass_kernel_spmd(nc, [arrays], core_ids=[0])
    return result.results[0]["out"].reshape(1, SEQ, D)
```
